# Optimizing a Trainium2 kernel written in Bass

```python
import jax, jax.numpy as jnp
from jax import lax
import numpy as np
import jax
import jax.numpy as jnp

D_MODEL = 2048
BATCH = 1
SEQ = 256
DEPTH = 1

HEAD_DIM = 128
D_MIX = D_MODEL
POOL_WIDTH = D_MIX // 4
N_POOL_GROUPS = 4
POOL_GROUP_DIM = POOL_WIDTH // N_POOL_GROUPS
POOL_WINDOWS = (2, 4, 8, 16)
ATTN_WIDTH = D_MIX // 2
N_ATTN_HEADS = ATTN_WIDTH // HEAD_DIM
LRU_WIDTH = D_MIX - POOL_WIDTH - ATTN_WIDTH
N_LRU_BLOCKS = 4
LRU_BLOCK_DIM = LRU_WIDTH // N_LRU_BLOCKS
LRU_CONV_WIDTH = 4
LRU_C = 8.0
D_FF = ((8 * D_MODEL // 3 + 255) // 256) * 256
FFN_CONV_WIDTH = 3
Q_BLOCK = 128
N_IN = POOL_WIDTH + 3 * ATTN_WIDTH + N_ATTN_HEADS + 2 * LRU_WIDTH
EPS = 1e-6


def rmsnorm(x, g):
    xf = x.astype(jnp.float32)
    y = xf * lax.rsqrt(jnp.mean(xf * xf, axis=-1, keepdims=True) + EPS)
    return (y * g.astype(jnp.float32)).astype(x.dtype)

def causal_dwconv(u, w, b):
    K = w.shape[0]
    S = u.shape[1]
    up = jnp.pad(u, ((0, 0), (K - 1, 0), (0, 0)))
    out = b + up[:, 0:S] * w[0]
    for k in range(1, K):
        out = out + up[:, k:k + S] * w[k]
    return out

def pool_mixer(u, w, scale):
    B, S, _ = u.shape
    uf = u.astype(jnp.float32).reshape(B, S, N_POOL_GROUPS, POOL_GROUP_DIM)
    cs = jnp.cumsum(uf, axis=1)
    pos = jnp.arange(1, S + 1, dtype=jnp.float32)
    outs = []
    for g, win in enumerate(POOL_WINDOWS):
        csg = cs[:, :, g]
        lag = jnp.pad(csg, ((0, 0), (win, 0), (0, 0)))[:, :S]
        mean = (csg - lag) / jnp.minimum(pos, float(win))[None, :, None]
        outs.append(mean - uf[:, :, g])
    d = jnp.stack(outs, axis=2).astype(u.dtype)
    y = jnp.einsum('bsgc,gcd->bsgd', d, w).reshape(B, S, POOL_WIDTH)
    return y * scale

def forgetting_attention(q, k, v, f_logit, b_f):
    B, S, _ = q.shape
    H = N_ATTN_HEADS
    q = q.reshape(B, S, H, HEAD_DIM).transpose(0, 2, 1, 3)
    k = k.reshape(B, S, H, HEAD_DIM).transpose(0, 2, 1, 3)
    v = v.reshape(B, S, H, HEAD_DIM).transpose(0, 2, 1, 3)
    log_f = jax.nn.log_sigmoid(f_logit.astype(jnp.float32) + b_f.astype(jnp.float32))
    F = jnp.cumsum(log_f, axis=1).transpose(0, 2, 1)
    nb = S // Q_BLOCK
    qb = q.reshape(B, H, nb, Q_BLOCK, HEAD_DIM).transpose(2, 0, 1, 3, 4)
    Fb = F.reshape(B, H, nb, Q_BLOCK).transpose(2, 0, 1, 3)
    kpos = jnp.arange(S)
    scale = HEAD_DIM ** -0.5

    def block(args):
        q_blk, F_blk, i = args
        qpos = i * Q_BLOCK + jnp.arange(Q_BLOCK)
        s = (jnp.einsum('bhqd,bhkd->bhqk', q_blk, k).astype(jnp.float32) * scale
             + F_blk[..., None] - F[:, :, None, :])
        s = jnp.where(kpos[None, :] <= qpos[:, None], s, -jnp.inf)
        p = jax.nn.softmax(s, axis=-1).astype(v.dtype)
        return jnp.einsum('bhqk,bhkd->bhqd', p, v)

    o = lax.map(block, (qb, Fb, jnp.arange(nb)))
    return o.transpose(1, 0, 3, 2, 4).reshape(B, S, H * HEAD_DIM)

def rg_lru_branch(xb, yb, conv_w, conv_b, wa, ba, wi, bi, lam):
    B, S, _ = xb.shape
    xc = causal_dwconv(xb, conv_w, conv_b)
    xh = xc.reshape(B, S, N_LRU_BLOCKS, LRU_BLOCK_DIM)
    gate_r = jax.nn.sigmoid((jnp.einsum('bshc,hcd->bshd', xh, wa).reshape(B, S, LRU_WIDTH) + ba).astype(jnp.float32))
    gate_i = jax.nn.sigmoid((jnp.einsum('bshc,hcd->bshd', xh, wi).reshape(B, S, LRU_WIDTH) + bi).astype(jnp.float32))
    log_a = -LRU_C * gate_r * jax.nn.softplus(-lam.astype(jnp.float32))
    a = jnp.exp(log_a)
    inp = jnp.sqrt(-jnp.expm1(2.0 * log_a)) * (gate_i * xc.astype(jnp.float32))

    def combine(left, right):
        a1, b1 = left
        a2, b2 = right
        return a1 * a2, a2 * b1 + b2

    _, h = lax.associative_scan(combine, (a, inp), axis=1)
    return (h * jax.nn.gelu(yb.astype(jnp.float32))).astype(xb.dtype)

def hybrid_mixer(h, w_in, b_f, pool_w, pool_scale, lru_conv_w, lru_conv_b,
                 lru_wa, lru_ba, lru_wi, lru_bi, lru_lambda, w_out):
    z = h @ w_in
    sizes = [POOL_WIDTH, ATTN_WIDTH, ATTN_WIDTH, ATTN_WIDTH, N_ATTN_HEADS, LRU_WIDTH]
    offsets = [int(o) for o in np.cumsum(sizes)]
    zp, zq, zk, zv, zf, zx, zy = jnp.split(z, offsets, axis=-1)
    y_pool = pool_mixer(zp, pool_w, pool_scale)
    y_attn = forgetting_attention(zq, zk, zv, zf, b_f)
    y_lru = rg_lru_branch(zx, zy, lru_conv_w, lru_conv_b, lru_wa, lru_ba, lru_wi, lru_bi, lru_lambda)
    y = jnp.concatenate([y_pool, y_attn.astype(h.dtype), y_lru], axis=-1)
    return y @ w_out

def conv_glu_ffn(h, w_gate, w_up, conv_w, conv_b, w_down):
    g = causal_dwconv(h @ w_gate, conv_w, conv_b)
    return (jax.nn.silu(g) * (h @ w_up)) @ w_down

def first_inputs(seed: int = 0) -> dict:
    key = jax.random.key(seed)
    ks = jax.random.split(key, 26)
    f32 = jnp.float32

    def nrm(k, shape, s):
        return jax.random.normal(k, shape, f32) * s

    u_lam = jax.random.uniform(ks[15], (DEPTH, LRU_WIDTH), f32, 0.9, 0.999)
    s_lam = u_lam ** (1.0 / LRU_C)
    lru_lambda = jnp.log(s_lam) - jnp.log1p(-s_lam)
    return {
        "x": nrm(ks[0], (BATCH, SEQ, D_MODEL), 1.0),
        "c": nrm(ks[1], (BATCH, D_MODEL), 1.0),
        "w_ada": nrm(ks[2], (DEPTH, D_MODEL, 6 * D_MODEL), 0.5 * D_MODEL ** -0.5),
        "b_ada": nrm(ks[3], (DEPTH, 6 * D_MODEL), 0.01),
        "g_mix": 1.0 + nrm(ks[4], (DEPTH, D_MODEL), 0.05),
        "w_in": nrm(ks[5], (DEPTH, D_MODEL, N_IN), D_MODEL ** -0.5),
        "b_f": jax.random.uniform(ks[6], (DEPTH, N_ATTN_HEADS), f32, 1.0, 5.0),
        "pool_w": nrm(ks[7], (DEPTH, N_POOL_GROUPS, POOL_GROUP_DIM, POOL_GROUP_DIM), POOL_GROUP_DIM ** -0.5),
        "pool_scale": 1.0 + nrm(ks[8], (DEPTH, POOL_WIDTH), 0.1),
        "lru_conv_w": nrm(ks[9], (DEPTH, LRU_CONV_WIDTH, LRU_WIDTH), LRU_CONV_WIDTH ** -0.5),
        "lru_conv_b": nrm(ks[10], (DEPTH, LRU_WIDTH), 0.01),
        "lru_wa": nrm(ks[11], (DEPTH, N_LRU_BLOCKS, LRU_BLOCK_DIM, LRU_BLOCK_DIM), LRU_BLOCK_DIM ** -0.5),
        "lru_ba": nrm(ks[12], (DEPTH, LRU_WIDTH), 0.01),
        "lru_wi": nrm(ks[13], (DEPTH, N_LRU_BLOCKS, LRU_BLOCK_DIM, LRU_BLOCK_DIM), LRU_BLOCK_DIM ** -0.5),
        "lru_bi": nrm(ks[14], (DEPTH, LRU_WIDTH), 0.01),
        "lru_lambda": lru_lambda,
        "w_out": nrm(ks[16], (DEPTH, D_MIX, D_MODEL), D_MIX ** -0.5),
        "g_ffn": 1.0 + nrm(ks[17], (DEPTH, D_MODEL), 0.05),
        "w_ffn_gate": nrm(ks[18], (DEPTH, D_MODEL, D_FF), D_MODEL ** -0.5),
        "w_ffn_up": nrm(ks[19], (DEPTH, D_MODEL, D_FF), D_MODEL ** -0.5),
        "ffn_conv_w": nrm(ks[20], (DEPTH, FFN_CONV_WIDTH, D_FF), FFN_CONV_WIDTH ** -0.5),
        "ffn_conv_b": nrm(ks[21], (DEPTH, D_FF), 0.01),
        "w_ffn_down": nrm(ks[22], (DEPTH, D_FF, D_MODEL), D_FF ** -0.5),
        "final_g": 1.0 + nrm(ks[23], (D_MODEL,), 0.05),
    }

def first_block(x, c, w_ada, b_ada, g_mix, w_in, b_f, pool_w, pool_scale, lru_conv_w, lru_conv_b,
              lru_wa, lru_ba, lru_wi, lru_bi, lru_lambda, w_out, g_ffn, w_ffn_gate, w_ffn_up,
              ffn_conv_w, ffn_conv_b, w_ffn_down, final_g):
    c_act = jax.nn.silu(c)
    for l in range(DEPTH):
        mod = c_act @ w_ada[l] + b_ada[l]
        sh1, sc1, gt1, sh2, sc2, gt2 = jnp.split(mod[:, None, :], 6, axis=-1)
        h = rmsnorm(x, g_mix[l]) * (1.0 + sc1) + sh1
        x = x + gt1 * hybrid_mixer(h, w_in[l], b_f[l], pool_w[l], pool_scale[l], lru_conv_w[l], lru_conv_b[l],
                                   lru_wa[l], lru_ba[l], lru_wi[l], lru_bi[l], lru_lambda[l], w_out[l])
        h = rmsnorm(x, g_ffn[l]) * (1.0 + sc2) + sh2
        x = x + gt2 * conv_glu_ffn(h, w_ffn_gate[l], w_ffn_up[l], ffn_conv_w[l], ffn_conv_b[l], w_ffn_down[l])
    return rmsnorm(x, final_g)


DEPTH_2 = 2

CHUNK = 64
N_MEM = 256
N_BRANCH = 4
BRANCH_WIDTH = D_MODEL // 4
N_HEADS = BRANCH_WIDTH // HEAD_DIM
IDX_HEADS = 8
IDX_DIM = 64
TOPK_MAX = 256
ROPE_BASE = 10000.0
W = BRANCH_WIDTH
SPLIT_SIZES = (W, W, W, W, IDX_HEADS * IDX_DIM, IDX_DIM, IDX_HEADS,
               W, W, W, W,
               W, W, W, W,
               W, W,
               N_BRANCH * D_MODEL)
IN_WIDTH = sum(SPLIT_SIZES)


def rms_norm(x, g):
    xf = x.astype(jnp.float32)
    y = xf * lax.rsqrt(jnp.mean(xf * xf, axis=-1, keepdims=True) + EPS)
    return (y * g.astype(jnp.float32)).astype(x.dtype)

def head_rms_norm(t, g):
    tf = t.astype(jnp.float32)
    y = tf * lax.rsqrt(jnp.mean(tf * tf, axis=-1, keepdims=True) + EPS)
    return (y * g.astype(jnp.float32)).astype(t.dtype)

def split_cols(u):
    parts = []
    off = 0
    for n in SPLIT_SIZES:
        parts.append(u[..., off:off + n])
        off += n
    return parts

def rope_tables(seq):
    inv = ROPE_BASE ** (-jnp.arange(0, HEAD_DIM, 2, dtype=jnp.float32) / HEAD_DIM)
    ang = jnp.arange(seq, dtype=jnp.float32)[:, None] * inv[None, :]
    return jnp.cos(ang), jnp.sin(ang)

def rope(t, cos, sin):
    half = HEAD_DIM // 2
    t1 = t[..., :half].astype(jnp.float32)
    t2 = t[..., half:].astype(jnp.float32)
    c, s = cos[:, None, :], sin[:, None, :]
    return jnp.concatenate([t1 * c - t2 * s, t1 * s + t2 * c], axis=-1).astype(t.dtype)

def sparse_index_attention(q, k, v, qi, ki, wi):
    B, S, H, Dh = q.shape
    n_sel = min(TOPK_MAX, S // 4)
    nb = S // Q_BLOCK
    key_chunk = jnp.arange(S) // CHUNK

    def to_blocks(t):
        return jnp.moveaxis(t.reshape(B, nb, Q_BLOCK, *t.shape[2:]), 1, 0)

    def block(args):
        start, qb, qib, wib = args
        q_chunk = (start + jnp.arange(Q_BLOCK)) // CHUNK
        visible = key_chunk[None, :] <= q_chunk[:, None]
        rel = jax.nn.relu(jnp.einsum('bqhd,bsd->bqhs', qib, ki).astype(jnp.float32) * IDX_DIM ** -0.5)
        score = jnp.einsum('bqh,bqhs->bqs', wib.astype(jnp.float32) * IDX_HEADS ** -0.5, rel)
        score = jnp.where(visible[None], score, -jnp.inf)
        _, sel = lax.top_k(score, n_sel)
        sel_ok = key_chunk[sel] <= q_chunk[None, :, None]
        ks = jax.vmap(lambda kk, ii: kk[ii])(k, sel)
        vs = jax.vmap(lambda vv, ii: vv[ii])(v, sel)
        logits = jnp.einsum('bqhd,bqkhd->bhqk', qb, ks).astype(jnp.float32) * HEAD_DIM ** -0.5
        logits = jnp.where(sel_ok[:, None], logits, -jnp.inf)
        p = jax.nn.softmax(logits, axis=-1).astype(vs.dtype)
        return jnp.einsum('bhqk,bqkhd->bqhd', p, vs)

    starts = jnp.arange(nb) * Q_BLOCK
    out = lax.map(block, (starts, to_blocks(q), to_blocks(qi), to_blocks(wi)))
    return jnp.moveaxis(out, 0, 1).reshape(B, S, H, Dh)

def retention(q, k, v):
    B, S, H, d = q.shape
    nc = S // CHUNK
    q = q.astype(jnp.float32).reshape(B, nc, CHUNK, H, d)
    k = k.astype(jnp.float32).reshape(B, nc, CHUNK, H, d)
    v = v.astype(jnp.float32).reshape(B, nc, CHUNK, H, d)
    log_g = jnp.log1p(-jnp.exp2(-5.0 - jnp.arange(H, dtype=jnp.float32)))
    pos = jnp.arange(CHUNK, dtype=jnp.float32)
    intra = jnp.exp(log_g[:, None, None] * jnp.abs(pos[:, None] - pos[None, :]))
    s = jnp.einsum('bnchd,bnehd->bnhce', q, k) * intra
    o_intra = jnp.einsum('bnhce,bnehd->bnchd', s, v)
    k_dec = k * jnp.exp(log_g[None, :] * (CHUNK - 1 - pos)[:, None])[:, :, None]
    kv = jnp.einsum('bnehd,bnehv->nbhdv', k_dec, v)
    chunk_decay = jnp.exp(log_g * CHUNK)[None, :, None, None]

    def step(state, kv_n):
        return chunk_decay * state + kv_n, state

    _, s_prev = lax.scan(step, jnp.zeros_like(kv[0]), kv)
    q_dec = q * jnp.exp(log_g[None, :] * (pos + 1.0)[:, None])[:, :, None]
    o_inter = jnp.einsum('bnchd,nbhdv->bnchv', q_dec, s_prev)
    return (o_intra + o_inter).reshape(B, S, H, d)

def hgrn2(f, i, q):
    B, S, H, d = q.shape
    nc = S // CHUNK
    f = f.astype(jnp.float32).reshape(B, nc, CHUNK, H, d)
    i = i.astype(jnp.float32).reshape(B, nc, CHUNK, H, d)
    q = q.astype(jnp.float32).reshape(B, nc, CHUNK, H, d)
    kin = 1.0 - f

    def tmaj(t):
        return jnp.moveaxis(t, 2, 0)

    def step(state, inp):
        f_t, k_t, i_t, q_t = inp
        state = f_t[..., None] * state + k_t[..., None] * i_t[..., None, :]
        return state, jnp.einsum('bnhd,bnhdv->bnhv', q_t, state)

    s0 = jnp.zeros((B, nc, H, d, d), jnp.float32)
    s_local, o_intra = lax.scan(step, s0, (tmaj(f), tmaj(kin), tmaj(i), tmaj(q)))
    o_intra = jnp.moveaxis(o_intra, 0, 2)
    cum = jnp.cumsum(jnp.log(f), axis=2)
    chunk_decay = jnp.exp(cum[:, :, -1])

    def cstep(state, inp):
        dec, sl = inp
        return dec[..., None] * state + sl, state

    _, s_prev = lax.scan(cstep, jnp.zeros((B, H, d, d), jnp.float32),
                         (jnp.moveaxis(chunk_decay, 1, 0), jnp.moveaxis(s_local, 1, 0)))
    o_inter = jnp.einsum('bnchd,nbhdv->bnchv', q * jnp.exp(cum), s_prev)
    return (o_intra + o_inter).reshape(B, S, H, d)

def memory_attention(q, mk, mv):
    logits = jnp.einsum('bshd,bmhd->bhsm', q, mk).astype(jnp.float32) * HEAD_DIM ** -0.5
    p = jax.nn.softmax(logits, axis=-1).astype(mv.dtype)
    return jnp.einsum('bhsm,bmhd->bshd', p, mv)

def hybrid_layer(x, mem, norm_g, w_in, qk_g, ret_g, hgrn_g, lb, w_mem_kv, w_branch, w_out, cos, sin):
    B, S, _ = x.shape
    dt = x.dtype
    h = rms_norm(x, norm_g)
    u = h @ w_in
    (a_q, a_k, a_v, a_z, a_qi, a_ki, a_wi,
     b_q, b_k, b_v, b_z,
     c_f, c_i, c_q, c_z,
     m_q, m_z, gates) = split_cols(u)

    def heads(t):
        return t.reshape(t.shape[0], t.shape[1], N_HEADS, HEAD_DIM)

    y_a = sparse_index_attention(head_rms_norm(heads(a_q), qk_g[0]), head_rms_norm(heads(a_k), qk_g[1]),
                                 heads(a_v), a_qi.reshape(B, S, IDX_HEADS, IDX_DIM), a_ki, a_wi)
    y_b = retention(rope(heads(b_q), cos, sin), rope(heads(b_k), cos, sin) * HEAD_DIM ** -0.5, heads(b_v))
    y_b = head_rms_norm(y_b, ret_g)
    f = lb + (1.0 - lb) * jax.nn.sigmoid(heads(c_f).astype(jnp.float32))
    y_c = head_rms_norm(hgrn2(f, heads(c_i), heads(c_q)), hgrn_g)
    mkv = mem @ w_mem_kv
    m_k, m_v = mkv[..., :W], mkv[..., W:]
    y_m = memory_attention(head_rms_norm(heads(m_q), qk_g[2]), head_rms_norm(heads(m_k), qk_g[3]), heads(m_v))

    gate_all = gates.reshape(B, S, N_BRANCH, D_MODEL)
    merged = jnp.zeros_like(x)
    for n, (y, z) in enumerate(((y_a, a_z), (y_b, b_z), (y_c, c_z), (y_m, m_z))):
        branch = y.reshape(B, S, W).astype(dt) * jax.nn.silu(z)
        merged = merged + jax.nn.sigmoid(gate_all[:, :, n]) * (branch @ w_branch[n])
    return x + merged @ w_out

def second_inputs(seed: int = 0) -> dict:
    key = jax.random.key(seed)
    ks = jax.random.split(key, 12)
    x = jax.random.normal(ks[0], (BATCH, SEQ, D_MODEL), jnp.float32)
    mem = jax.random.normal(ks[1], (BATCH, N_MEM, D_MODEL), jnp.float32)
    norm_g = 1.0 + 0.02 * jax.random.normal(ks[2], (DEPTH_2, D_MODEL), jnp.float32)
    w_in = jax.random.normal(ks[3], (DEPTH_2, D_MODEL, IN_WIDTH), jnp.float32) * D_MODEL ** -0.5
    qk_norm_g = 1.0 + 0.02 * jax.random.normal(ks[4], (DEPTH_2, 4, HEAD_DIM), jnp.float32)
    ret_norm_g = 1.0 + 0.02 * jax.random.normal(ks[5], (DEPTH_2, N_HEADS, HEAD_DIM), jnp.float32)
    hgrn_norm_g = 1.0 + 0.02 * jax.random.normal(ks[6], (DEPTH_2, N_HEADS, HEAD_DIM), jnp.float32)
    lb_logits = 0.5 * jax.random.normal(ks[7], (DEPTH_2, N_HEADS, HEAD_DIM), jnp.float32)
    w_mem_kv = jax.random.normal(ks[8], (DEPTH_2, D_MODEL, 2 * W), jnp.float32) * D_MODEL ** -0.5
    w_branch = jax.random.normal(ks[9], (DEPTH_2, N_BRANCH, W, D_MODEL), jnp.float32) * W ** -0.5
    w_out = jax.random.normal(ks[10], (DEPTH_2, D_MODEL, D_MODEL), jnp.float32) * D_MODEL ** -0.5
    return {'x': x, 'mem': mem, 'norm_g': norm_g, 'w_in': w_in, 'qk_norm_g': qk_norm_g,
            'ret_norm_g': ret_norm_g, 'hgrn_norm_g': hgrn_norm_g, 'lb_logits': lb_logits,
            'w_mem_kv': w_mem_kv, 'w_branch': w_branch, 'w_out': w_out}

def second_block(x, mem, norm_g, w_in, qk_norm_g, ret_norm_g, hgrn_norm_g, lb_logits, w_mem_kv, w_branch, w_out):
    seq = x.shape[1]
    p = jax.nn.softmax(lb_logits.astype(jnp.float32), axis=0)
    lower_bounds = jnp.cumsum(p, axis=0) - p[0:1]
    cos, sin = rope_tables(seq)
    for l in range(DEPTH_2):
        x = hybrid_layer(x, mem, norm_g[l], w_in[l], qk_norm_g[l], ret_norm_g[l], hgrn_norm_g[l],
                         lower_bounds[l], w_mem_kv[l], w_branch[l], w_out[l], cos, sin)
    return x


def setup_inputs(seed=0):
    out = dict(first_inputs(seed))
    for name, value in second_inputs(seed + 1).items():
        if name != "x":
            out[name + "_2"] = value
    return out


def reference(
    x, c, w_ada, b_ada, g_mix, w_in, b_f, pool_w, pool_scale, lru_conv_w, lru_conv_b, lru_wa,
    lru_ba, lru_wi, lru_bi, lru_lambda, w_out, g_ffn, w_ffn_gate, w_ffn_up, ffn_conv_w,
    ffn_conv_b, w_ffn_down, final_g, mem_2, norm_g_2, w_in_2, qk_norm_g_2, ret_norm_g_2,
    hgrn_norm_g_2, lb_logits_2, w_mem_kv_2, w_branch_2, w_out_2,
):
    x = first_block(
        x, c, w_ada, b_ada, g_mix, w_in, b_f, pool_w, pool_scale, lru_conv_w, lru_conv_b,
        lru_wa, lru_ba, lru_wi, lru_bi, lru_lambda, w_out, g_ffn, w_ffn_gate, w_ffn_up,
        ffn_conv_w, ffn_conv_b, w_ffn_down, final_g,
    )
    return second_block(
        x, mem_2, norm_g_2, w_in_2, qk_norm_g_2, ret_norm_g_2, hgrn_norm_g_2, lb_logits_2,
        w_mem_kv_2, w_branch_2, w_out_2,
    )


_drawn_inputs = setup_inputs


def setup_inputs(seed=0):
    import zlib

    import numpy as np

    out = dict(_drawn_inputs(seed))
    spreads = {}
    factors = {'lru_conv_b': 4.928,
     'lru_ba': 23.192,
     'lru_bi': 8.0,
     'ffn_conv_b': 7.256,
     'qk_norm_g_2': 8.0,
     'ret_norm_g_2': 5.935,
     'hgrn_norm_g_2': 5.833}
    for name, (base, spread) in spreads.items():
        noise = np.random.default_rng([zlib.crc32(name.encode()), seed]).standard_normal(out[name].shape)
        drawn = base * np.exp(spread * noise) if base else spread * noise
        out[name] = jnp.asarray(drawn.astype(out[name].dtype))
    for name, factor in factors.items():
        out[name] = (out[name] * factor).astype(out[name].dtype)
    return out
```

```python
from contextlib import ExitStack

import numpy as np

import concourse.bass as bass
from concourse import mybir

F32 = mybir.dt.float32
F32R = mybir.dt.float32r
ALU = mybir.AluOpType
ACT = mybir.ActivationFunctionType
AX = mybir.AxisListType

P = 128
S = 256
TB = S // P
D = 2048
KD = D // P
NW = 512
NB = D // NW
KC = 2
GT = KD // KC
RING = 4
HD = 128
NH = 4
FF = 5632
NFF = FF // NW
ADA = 6 * D
AQ = D
ADA_RING = 4
NQ = ADA // AQ
LAYERS = 2
SUB = 16
NSUB = S // SUB
IDX_HEADS = 8
IDX_DIM = 64
NSEL = 64
ROUNDS = NSEL // 8
SMALL = IDX_DIM + IDX_HEADS
CHUNK = 64
EPS = 1e-6
HIDDEN = -3.0e38
TAKEN = -3.4e38
FAR = -1.0e30
POOL_WINDOWS = (2, 4, 8, 16)
SCALE = float(HD) ** -0.5

G_MEM = 0
G_IN = G_MEM + 2 * LAYERS
G_OUT = G_IN + 9
G_FF = G_OUT + NB
G_LAYER = G_FF + 3 * NFF
IN2 = 15
PER_LAYER = IN2 + 5 * NB + NB
GROUPS = G_LAYER + LAYERS * PER_LAYER

VEC = {}
_at = 0
for _name, _n in (("c", KD), ("g_mix", KD), ("g_ffn", KD), ("final_g", KD), ("pool_scale", 4),
                  ("conv_w", 16), ("conv_b", 4), ("ba", 4), ("bi", 4), ("lam", 4),
                  ("ffn_w", 3 * FF // P), ("ffn_b", FF // P), ("lb", LAYERS * NH),
                  ("mk_g", LAYERS), ("b_ada", ADA // P)):
    VEC[_name] = (_at, _at + _n)
    _at += _n
NVEC = _at
LVEC = {"norm_g": (0, KD), "qk_g": (KD, KD + 4), "ret_g": (KD + 4, KD + 8), "hgrn_g": (KD + 8, KD + 12)}
NLVEC = KD + 12
CON = {}
_at = 0
for _name, _n in (("ident", P), ("ones", P), ("sel", P + SUB), ("decay", 2 * NH * P), ("visible", TB * S),
                  ("same", P), ("cos", TB * 64), ("sin", TB * 64)):
    CON[_name] = (_at, _at + _n)
    _at += _n
NCON = _at
CON1 = {}
_at = 0
for _name, _n in (("causal", TB * S), ("tri", TB * S), ("row", 8 * P)):
    CON1[_name] = (_at, _at + _n)
    _at += _n
NCON1 = _at


class Steps:

    def __init__(self, eng, sem):
        self.eng, self.sem, self.base, self.count, self.outer = eng, sem, 0, 0, []

    def __call__(self, ins):
        ins.then_inc(self.sem, 1)
        self.count += 1

    def settle(self):
        self.eng.wait_ge(self.sem, self.base + self.count)

    def enter(self, index, per):
        self.outer.append((self.base, self.count))
        self.base = self.base + self.count + index * per
        self.count = 0

    def leave(self, trips, per):
        assert self.count == per, (self.count, per)
        base, count = self.outer.pop()
        self.base, self.count = base, count + trips * per


def build(nc, t):
    with ExitStack() as ctx:
        def sb(name, shape, dt=F32):
            return ctx.enter_context(nc.sbuf_tensor(name, shape, dt))

        def sem(name):
            return ctx.enter_context(nc.semaphore(name))

        x = sb("x_rows", [P, TB, D])
        hT_hi = sb("hT_hi", [P, KD, S], F32R)
        hT_lo = sb("hT_lo", [P, KD, S], F32R)
        raw = sb("w_raw", [P, RING, KC * NW])
        w_hi = sb("w_hi", [P, RING, KC, NW], F32R)
        w_lo = sb("w_lo", [P, RING, KC, NW], F32R)
        r_at = nc.sbuf_base
        R = sb("R", [P, 19456])
        yr = nc.alloc_sbuf_tensor_at("y_parts", [P, 9216], F32R, offset=r_at + 40 * 1024)
        mk_T = sb("mk_T", [P, LAYERS, NH, S])
        mv = sb("mv", [P, LAYERS, TB, NW])
        small_w = sb("small_w_sb", [P, KD * SMALL])
        con = sb("con_sb", [P, NCON])
        vec = sb("vec_sb", [P, NVEC])
        lvec = sb("lvec_sb", [P, NLVEC])
        mod = sb("mod", [P, ADA // P])
        sc = sb("sc", [P, 304])
        pg = [ctx.enter_context(nc.psum_tensor(f"pg{b}", [P, TB, NW], F32)) for b in range(2)]
        pm = [ctx.enter_context(nc.psum_tensor(f"pm{b}", [P, NW], F32)) for b in range(4)]

        def view(kb, *dims):
            n = int(np.prod(dims))
            assert int(kb * 256) + n <= 19456
            v = R[:, int(kb * 256):int(kb * 256) + n]
            names = "abcd"[:len(dims)]
            if len(dims) == 1:
                return v
            return v.rearrange(f"p ({' '.join(names)}) -> p {' '.join(names)}",
                               **{k: d for k, d in zip(names[1:], dims[1:])})

        def view_r(kb, *dims):
            n = int(np.prod(dims))
            v = yr[:, int(kb - 40) * 256:int(kb - 40) * 256 + n]
            names = "abcd"[:len(dims)]
            return v.rearrange(f"p ({' '.join(names)}) -> p {' '.join(names)}",
                               **{k: d for k, d in zip(names[1:], dims[1:])})

        def flat(v):
            names = "abcd"[:len(v.shape) - 1]
            return v.rearrange(f"p {' '.join(names)} -> p ({' '.join(names)})")

        def V(name):
            return vec[:, VEC[name][0]:VEC[name][1]]

        def LV(name):
            return lvec[:, LVEC[name][0]:LVEC[name][1]]

        def C(name):
            return con[:, CON[name][0]:CON[name][1]]

        ident, ones, sel, same = C("ident"), C("ones"), C("sel"), C("same")
        decay = C("decay").rearrange("p (a h t) -> p a h t", a=2, h=NH)
        visible = C("visible").rearrange("p (a s) -> p a s", a=TB)
        cos = C("cos").rearrange("p (a d) -> p a d", a=TB)
        sin = C("sin").rearrange("p (a d) -> p a d", a=TB)
        c_act = sc[:, 0:16]
        ssq = sc[:, 16:18]
        rstd = sc[:, 18:20]
        nmax = sc[:, 20:28]
        psum_of = sc[:, 28:36]
        rsum = sc[:, 36:44]
        hss = sc[:, 44:60]
        hrs = sc[:, 60:76]
        spl = sc[:, 76:84]
        lb = sc[:, 84:92]
        lbc = sc[:, 92:96]
        oml = sc[:, 96:100]
        gq = sc[:, 100:102]
        t8 = sc[:, 104:136]
        top8 = sc[:, 136:152]
        wi = sc[:, 216:232]
        F_end = sc[:, 152:216]

        mem_f = view(0, KD, S)
        mk_tok = view(16, TB, NW)
        mk_sq = view(20, TB, NW)
        hf_1 = view(0, KD, S)
        xn_1 = view(16, TB, D)
        ada_ring = view(36, ADA_RING, AQ)
        ada_acc = view(68, AQ)
        xn = view(60, TB, D)
        hf = view(44, KD, S)
        Z = view(0, 9, TB, NW)
        YT = view(36, KD, S)
        band = view(40, TB, 4, S)
        con1 = view(52, NCON1)
        causal = con1[:, 0:TB * S].rearrange("p (a s) -> p a s", a=TB)
        tri = con1[:, TB * S:2 * TB * S].rearrange("p (a s) -> p a s", a=TB)
        row = con1[:, 2 * TB * S:].rearrange("p (h s) -> p h s", h=8)
        pool_w = view(60, 4, P)
        QK1 = view(62, 2, NH, S)
        pool_d = view(70, 4, S)
        o1 = view(70, TB, NW)
        zf, logf, F_t = (sc[:, 240 + 16 * i:256 + 16 * i].rearrange("p (a h) -> p a h", a=TB) for i in range(3))
        b_f = sc[:, 288:296]
        F_row = view(75, S)
        w_f = small_w[:, 0:KD * 8].rearrange("p (k n) -> p k n", n=8)
        lru_w = small_w[:, KD * 8:KD * 8 + 2 * 4 * P].rearrange("p (g b n) -> p g b n", g=2, b=4)
        X_, GR, GI, A_, TH, Y_ = [view(4 * i, 4, S) for i in range(6)]
        gate_b = view(0, D)
        dg1 = view(8, KD, P)
        dg3 = view(24, KD, P)
        o_tmp = view(48, TB, NW)
        F_acc = view(8, NB, TB, NW)
        g_tok = view(24, TB, NW)
        u_tok = view(28, TB, NW)
        g_cv = view(32, 4, S)
        a_f = view(36, 4, S)
        aT_hi = view_r(40, 4, S)
        aT_lo = view_r(44, 4, S)
        junk = view(32, TB, D)
        U = view(0, 5, TB, NW)
        yT_hi = view_r(44, 4, 4, S)
        yT_lo = view_r(60, 4, 4, S)
        QK2 = view(20, 2, NH, S)
        small_u = view(28, TB, SMALL)
        kiT = view(29, S)
        qiT = view(30, 4, S)
        ki2 = view(34, TB, P)
        rel = view(34, 2, TB, S)
        score = view(38, TB, S)
        br_f = view(40, 4, S)
        rows_b = view(28, 2, TB, NW)
        rope_t = view(36, TB, NW)
        T = [view(16 + 4 * i, NH, S) for i in range(7)]
        T0, T2 = view(0, NH, S), view(8, NH, S)
        sg = view(0, 4, TB, NW)
        merged = view(16, TB, D)
        m_tmp = view(32, TB, NW)
        hf_m = view(0, KD, S)

        def sections_as_scores(kb):
            return view(kb, NH, TB, S)

        consts_in, cons1_in, x_in, mem_in, lw_in = map(sem, ("consts_in", "cons1_in", "x_in", "mem_in", "lw_in"))
        ada_in = [sem(f"ada_in{i}") for i in range(ADA_RING)]
        raw_in = [sem(f"raw_in{i}") for i in range(RING)]
        out_stored = sem("out_stored")
        hi_done, lo_done, tile_used = map(sem, ("hi_done", "lo_done", "tile_used"))
        evac_act, evac_dve = map(sem, ("evac_act", "evac_dve"))
        dve_step, act_step = map(sem, ("dve_step", "act_step"))
        section = sem("section")
        waited = sem("waited")
        c_ready, ada_used, mod_ps, mod_taken = map(sem, ("c_ready", "ada_used", "mod_ps", "mod_taken"))
        memT_ready = sem("memT_ready")
        ssq_done, var_done, std_done = map(sem, ("ssq_done", "var_done", "std_done"))
        rows_ready, rowsT_ps, hf_done, hT_ready = map(sem, ("rows_ready", "rowsT_ps", "hf_done", "hT_ready"))
        hss_done, hstd_done, hn_ready = map(sem, ("hss_done", "hstd_done", "hn_ready"))
        T_ps, T_sb = map(sem, ("T_ps", "T_sb"))
        logit_ps, max_done, exp_done, P_T_ps, P_T_sb, o_ps = map(
            sem, ("logit_ps", "max_done", "exp_done", "P_T_ps", "P_T_sb", "o_ps"))
        silu_done, y_ready, y_T_ps, y_T_sb, y_split = map(
            sem, ("silu_done", "y_ready", "y_T_ps", "y_T_sb", "y_split"))
        bc_dg, bc_ps, bc_done = map(sem, ("bc_dg", "bc_ps", "bc_done"))
        lam_in, lam_out = map(sem, ("lam_in", "lam_out"))
        zf_ps, zf_in, zf_out, logf_ready, F_ps, F_sb = map(
            sem, ("zf_ps", "zf_in", "zf_out", "logf_ready", "F_ps", "F_sb"))
        pool_ps, pool_sb = map(sem, ("pool_ps", "pool_sb"))
        lru_ps, lru_act, lru_dve = map(sem, ("lru_ps", "lru_act", "lru_dve"))
        ff_ps, ff_tap, ff_conv, ff_silu, aT_ready = map(
            sem, ("ff_ps", "ff_tap", "ff_conv", "ff_silu", "aT_ready"))
        small_ps, small_sb, idx_ps, idx_sb, rel_ps, rel_sb, rel_used = map(
            sem, ("small_ps", "small_sb", "idx_ps", "idx_sb", "rel_ps", "rel_sb", "rel_used"))
        rope_done, ret_ps, ret_sb = map(sem, ("rope_done", "ret_ps", "ret_sb"))
        fq_ps, fq_sb, W_ready, W_used, K_ready, A_ps, A_sb = map(
            sem, ("fq_ps", "fq_sb", "W_ready", "W_used", "K_ready", "A_ps", "A_sb"))

        block = ctx.enter_context(nc.Block())

        END_MEM0, END_MEM1, END_ADA, END_NORM1, END_MIX, END_OUT1, END_NORM2, END_FF, END_B1 = range(1, 10)
        END_NORM, END_A, END_B, END_C, END_M, END_LAYER = range(1, 7)
        PER_END = 6
        A_IN, A_FF, A_L, A_PER = 4, 13, 13 + 2 * NFF, IN2 + 16
        V_OUT, V_FF, V_L, V_PER = 2, 2 + NB, 2 + NB + NB * NFF, 16 + NB
        L_B, L_C, L_M, L_G, L_O = 5, 9, 13, 15, 35
        LAYER_STEPS = 241
        HN0, HN = 2, 4
        AT0, AT = 2, 2

        @block.sync
        def _(sp):
            sp.dma_start(con[:, :], t["con"]).then_inc(consts_in, 16)
            sp.dma_start(vec[:, :], t["vec"]).then_inc(consts_in, 16)
            sp.dma_start(b_f, t["b_f"].partition_broadcast(P)).then_inc(consts_in, 16)
            sp.dma_start(mem_f, t["mem_T"]).then_inc(mem_in, 16)
            sp.dma_start(x[:, :, :], t["x"]).then_inc(x_in, 16)

            def tiles(group, first=False, count=GT):
                for g in range(count):
                    if not (first and g < RING):
                        sp.wait_ge(lo_done, group * GT + g - RING + 1)
                    sp.dma_start(raw[:, g % RING, :],
                                 t["w"][bass.ds(group * GT + g, 1), :, :].rearrange("o p n -> (o p) n")
                                 ).then_inc(raw_in[g % RING], 16)

            tiles(0, True)
            with sp.Fori(1, GROUPS) as group:
                tiles(group)
            tiles(GROUPS, count=RING)
            sp.wait_ge(section, END_B1 + LAYERS * PER_END)
            sp.dma_start(t["out"], x[:, :, :]).then_inc(out_stored, 16)
            sp.wait_ge(out_stored, 16)

        @block.gpsimd
        def _(pool):
            pool.dma_start(w_f, t["w_f"]).then_inc(lw_in, 16)
            with pool.Fori(0, NQ) as q:
                with pool.Fori(0, KD // ADA_RING) as kk:
                    for i in range(ADA_RING):
                        pool.wait_ge(ada_used, q * KD + kk * ADA_RING + i + 1)
                        pool.dma_start(ada_ring[:, i, :],
                                       t["w_ada"][bass.ds(kk * ADA_RING + i, 1), :, bass.ds(q * AQ, AQ)]
                                       .rearrange("o p n -> (o p) n")).then_inc(ada_in[i], 16)
            pool.wait_ge(mod_ps, NQ)
            pool.wait_ge(zf_ps, 1)
            pool.dma_start(con1, t["con1"]).then_inc(cons1_in, 16)
            pool.dma_start(pool_w, t["pool_w"]).then_inc(cons1_in, 16)
            pool.dma_start(band, t["band"]).then_inc(cons1_in, 16)
            pool.dma_start(lru_w, t["lru_w"]).then_inc(cons1_in, 16)
            with pool.Fori(0, LAYERS) as l:
                pool.wait_ge(section, END_B1 + l * PER_END)
                pool.dma_start(small_w[:, :], t["small_w"][bass.ds(l, 1), :, :].rearrange("o p n -> (o p) n")
                               ).then_inc(lw_in, 16)
                pool.dma_start(lvec[:, :], t["lvec"][bass.ds(l, 1), :, :].rearrange("o p n -> (o p) n")
                               ).then_inc(lw_in, 16)

        @block.scalar
        def _(act):
            def split(group, tiles, first=False):
                for g in tiles:
                    act.wait_ge(raw_in[g % RING], 16 * (group * (GT // RING) + g // RING + 1))
                    if not first:
                        act.wait_ge(tile_used, group * GT + g - RING + 1)
                    act.activation(w_hi[:, g % RING, :, :].rearrange("p c n -> p (c n)"), raw[:, g % RING, :],
                                   ACT.Copy).then_inc(hi_done, 1)

            def take(group, b, dest, func=ACT.Copy):
                act.wait_ge(tile_used, (group + 1) * GT)
                act.activation(dest, flat(pg[b][:, :, :]), func).then_inc(evac_act, 1)

            def advance(group):
                split(group, range(4, GT))
                split(group + 1, range(4))

            def columns(base, n, dest, func=ACT.Copy):
                with act.Fori(0, n // 2) as j:
                    for i in range(2):
                        advance(base + j * 2 + i)
                        take(base + j * 2 + i, i, dest(j * 2 + i), func)
                if n % 2:
                    advance(base + n - 1)
                    take(base + n - 1, 0, dest(n - 1), func)

            def transposed(occ, dest, gain=None, bias=None):
                for q in range(GT):
                    act.wait_ge(rowsT_ps, occ * GT + q + 1)
                    for c in range(KC):
                        k = q * KC + c
                        src = pm[q % 4][:, c * S:(c + 1) * S]
                        if gain is None:
                            i = act.activation(dest[:, k, :], src, ACT.Copy)
                        elif bias is None:
                            i = act.activation(dest[:, k, :], src, ACT.Copy, scale=gain[:, k:k + 1])
                        else:
                            i = act.activation(dest[:, k, :], src, ACT.Identity, bias=bias[:, k:k + 1],
                                               scale=gain[:, k:k + 1])
                    i.then_inc(hf_done, 1)

            def squares(occ, out):
                for tb in range(TB):
                    act.activation(out[:, tb, :], x[:, tb, :], ACT.Square,
                                   accum_out=ssq[:, tb:tb + 1]).then_inc(ssq_done, 1)
                act.wait_ge(var_done, occ + 1)
                act.activation(rstd, ssq, ACT.Sqrt).then_inc(std_done, 1)

            def head_std(occ, n):
                act.wait_ge(hss_done, occ + 1)
                act.activation(hrs[:, 0:n], hss[:, 0:n], ACT.Sqrt).then_inc(hstd_done, 1)

            def attn(occ, S_, PT):
                for h in range(NH):
                    act.wait_ge(max_done, occ * NH + h + 1)
                    for tb in range(TB):
                        i = act.activation(S_[:, h, tb, :], S_[:, h, tb, :], ACT.Exp,
                                           bias=nmax[:, 2 * h + tb:2 * h + tb + 1],
                                           accum_out=psum_of[:, 2 * h + tb:2 * h + tb + 1])
                    i.then_inc(exp_done, 1)
                for h in range(NH):
                    act.wait_ge(P_T_ps, occ * NH + h + 1)
                    act.activation(flat(PT[:, h, :, :]), pm[h][:, :], ACT.Copy).then_inc(P_T_sb, 1)

            def y_transposed(occ, dest, gain=None):
                for q in range(2):
                    act.wait_ge(y_T_ps, occ * 2 + q + 1)
                    for c in range(2):
                        k = 2 * q + c
                        i = act.activation(dest[:, k, :], pm[2 + q][:, c * S:(c + 1) * S], ACT.Copy,
                                           scale=1.0 if gain is None else gain[:, k:k + 1])
                    i.then_inc(y_T_sb, 1)

            def heads_T(value, banks, dest, scale=1.0):
                for i, b in enumerate(banks):
                    act.wait_ge(T_ps, value + i + 1)
                    act.activation(flat(dest[:, 2 * i:2 * i + 2, :]), pm[b][:, :], ACT.Copy,
                                   scale=scale).then_inc(T_sb, 1)

            act.wait_ge(consts_in, 48)
            act.activation(c_act, V("c"), ACT.Silu).then_inc(c_ready, 1)

            split(0, range(4), first=True)
            for l in range(LAYERS):
                g0 = G_MEM + 2 * l
                advance(g0)
                if l:
                    act.wait_ge(section, END_MEM0)
                take(g0, 0, flat(mk_tok))
                advance(g0 + 1)
                take(g0 + 1, 1, flat(mv[:, l, :, :]))
                head_std(l, 8)
                heads_T(2 * l, (2, 3), mk_T[:, l, :, :], scale=V("mk_g")[:, l:l + 1])

            act.wait_ge(x_in, 16)
            act.wait_ge(section, END_MEM1)
            squares(0, xn_1)
            act.wait_ge(section, END_ADA)
            transposed(0, hf_1, gain=mod[:, 16:32], bias=mod[:, 0:16])
            act.wait_ge(lam_in, 1)
            act.activation(t8[:, 4:12], t8[:, 4:12], ACT.Exp).then_inc(lam_out, 1)
            act.activation(spl[:, 0:4], spl[:, 4:8], ACT.Exp).then_inc(lam_out, 1)
            act.wait_ge(lam_out, 2)
            act.activation(spl[:, 0:4], spl[:, 0:4], ACT.Ln, bias=1.0).then_inc(lam_out, 1)
            columns(G_IN, 9, lambda j: Z[:, bass.ds(j, 1), :, :].rearrange("p o a n -> p (o a n)"))

            act.wait_ge(zf_in, 1)
            act.activation(flat(logf), flat(logf), ACT.Exp).then_inc(zf_out, 1)
            act.wait_ge(zf_out, 1)
            act.activation(flat(logf), flat(logf), ACT.Ln, bias=1.0).then_inc(zf_out, 1)
            act.wait_ge(F_ps, 1)
            act.activation(F_row[0:8, :], pm[0][0:8, 0:S], ACT.Copy, scale=-1.0).then_inc(F_sb, 1)
            act.activation(flat(F_t), pm[0][:, S:S + TB * 8], ACT.Copy).then_inc(F_sb, 1)
            for q in range(2):
                act.wait_ge(pool_ps, q + 1)
                act.activation(flat(pool_d[:, 2 * q:2 * q + 2, :]), pm[2 + q][:, :],
                               ACT.Copy).then_inc(pool_sb, 1)
            for q in range(2):
                act.wait_ge(pool_ps, q + 3)
                for c in range(2):
                    g = 2 * q + c
                    i = act.activation(YT[:, g, :], pm[q][:, c * S:(c + 1) * S], ACT.Copy,
                                       scale=V("pool_scale")[:, g:g + 1])
                i.then_inc(pool_sb, 1)
            for b in range(2):
                heads_T(4 + 4 * b, (0, 1), QK1[:, 0, :, :], scale=SCALE)
                heads_T(6 + 4 * b, (2, 3), QK1[:, 1, :, :])
                attn(b, sections_as_scores(12 * b), QK1.rearrange("p q h s -> p (q h s)")
                     .rearrange("p (h a s) -> p h a s", h=NH, a=TB))
                y_transposed(b, YT[:, 4 + 4 * b:8 + 4 * b, :])
            act.wait_ge(lru_dve, 1)
            for q in range(2):
                act.wait_ge(lru_ps, q + 1)
                for c in range(2):
                    b = 2 * q + c
                    i = act.activation(X_[:, b, :], pm[q][:, c * S:(c + 1) * S], ACT.Identity,
                                       bias=V("conv_b")[:, b:b + 1], scale=V("conv_w")[:, 4 * b + 3:4 * b + 4])
                i.then_inc(lru_act, 1)
            for q in range(2):
                act.wait_ge(lru_ps, q + 3)
                act.activation(flat(Y_)[:, q * NW:(q + 1) * NW], pm[2 + q][:, :], ACT.Copy).then_inc(lru_act, 1)
            for gate, (dst, bias) in enumerate(((GR, "ba"), (GI, "bi"))):
                act.wait_ge(lru_ps, gate + 5)
                for b in range(4):
                    i = act.activation(dst[:, b, :], pm[2 * gate + b // 2][:, (b % 2) * S:(b % 2 + 1) * S],
                                       ACT.Sigmoid, bias=V(bias)[:, b:b + 1])
                i.then_inc(lru_act, 1)
            act.wait_ge(lru_dve, 3)
            act.activation(flat(A_), flat(GR), ACT.Exp).then_inc(lru_act, 1)
            act.activation(flat(TH), flat(GR), ACT.Tanh, scale=-1.0).then_inc(lru_act, 1)
            act.wait_ge(lru_dve, 4)
            act.activation(flat(TH), flat(TH), ACT.Sqrt).then_inc(lru_act, 1)
            act.wait_ge(lru_dve, 5)
            act.activation(flat(GR), flat(GR), ACT.Tanh, scale=0.7978845608028654).then_inc(lru_act, 1)

            def broadcast(occ):
                for n in range(NB):
                    act.wait_ge(bc_ps, occ * NB + n + 1)
                    act.activation(gate_b[:, n * NW:(n + 1) * NW], pm[n][:, :], ACT.Copy).then_inc(bc_done, 1)

            broadcast(0)
            with act.Fori(0, NB) as j:
                advance(G_OUT + j)
            act.wait_ge(section, END_OUT1)
            squares(1, xn)
            transposed(1, hf, gain=mod[:, 64:80], bias=mod[:, 48:64])
            broadcast(1)

            def ff_col(name, j, k, n, at=0):
                return vec[:, bass.ds(VEC[name][0] + (j * 4 + k) * n + at, 1)]

            def tap(j):
                for q in range(2):
                    act.wait_ge(ff_ps, j * 4 + q + 1)
                    for c in range(2):
                        k = 2 * q + c
                        i = act.activation(g_cv[:, k, :], pm[q][:, c * S:(c + 1) * S], ACT.Identity,
                                           bias=ff_col("ffn_b", j, k, 1), scale=ff_col("ffn_w", j, k, 3, 2))
                    i.then_inc(ff_tap, 1)

            def silu(j):
                act.wait_ge(ff_conv, j + 1)
                act.activation(flat(g_cv), flat(g_cv), ACT.Silu).then_inc(ff_silu, 1)

            act.wait_ge(section, END_NORM2)
            advance(G_FF)
            take(G_FF, 0, flat(g_tok))
            advance(G_FF + 1)
            take(G_FF + 1, 1, flat(u_tok))
            with act.Fori(0, NFF - 1) as j:
                g0 = G_FF + 2 + j * 3
                advance(g0)
                tap(j)
                act.wait_ge(ff_ps, j * 4 + 4)
                take(g0, 0, flat(g_tok))
                split(g0 + 1, range(4, 6))
                silu(j)
                split(g0 + 1, range(6, 8))
                split(g0 + 2, range(4))
                take(g0 + 1, 1, flat(u_tok))
                advance(g0 + 2)
            tap(NFF - 1)
            silu(NFF - 1)
            advance(G_FF + 3 * NFF - 1)
            act.wait_ge(section, END_FF)
            broadcast(2)
            squares(2, junk)

            with act.Fori(0, LAYERS) as l:
                base = G_LAYER + l * PER_LAYER
                end = END_B1 + l * PER_END
                evac0 = A_L + l * A_PER
                act.wait_ge(section, end)
                squares(3 + l, xn)
                act.wait_ge(lw_in, 16 * (3 + 2 * l))
                transposed(2 + l * 2, hf, gain=LV("norm_g"))
                act.wait_ge(small_ps, l + 1)
                act.activation(flat(small_u), pm[0][:, 0:TB * SMALL], ACT.Copy).then_inc(small_sb, 1)
                act.wait_ge(section, end + END_NORM)

                def section_of(j):
                    return U[:, bass.ds(j, 1), :, :].rearrange("p o a n -> p (o a n)")

                columns(base, 5, section_of)
                head_std(HN0 + l * HN, 16)
                for i in range(2):
                    act.wait_ge(idx_ps, l * 3 + i + 1)
                    act.activation(flat(qiT[:, 2 * i:2 * i + 2, :]), pm[i][:, :], ACT.Copy).then_inc(idx_sb, 1)
                act.wait_ge(idx_ps, l * 3 + 3)
                act.activation(kiT, pm[2][:, 0:S], ACT.Copy).then_inc(idx_sb, 1)
                for h in range(IDX_HEADS):
                    act.wait_ge(rel_ps, l * IDX_HEADS + h + 1)
                    if h >= 2:
                        act.wait_ge(rel_used, l * IDX_HEADS + h - 1)
                    act.activation(flat(rel[:, h % 2, :, :]), pm[h % 4][:, :], ACT.Relu,
                                   scale=float(IDX_DIM) ** -0.5).then_inc(rel_sb, 1)
                tb0 = 12 + l * 14
                heads_T(tb0, (0, 1), QK2[:, 0, :, :], scale=gq[:, 0:1])
                heads_T(tb0 + 2, (2, 3), QK2[:, 1, :, :], scale=LV("qk_g")[:, 1:2])
                attn(AT0 + l * AT, sections_as_scores(0), view(20, NH, TB, S))
                act.wait_ge(evac_act, evac0 + 5)
                act.activation(flat(U[:, 3, :, :]), flat(U[:, 3, :, :]), ACT.Silu).then_inc(silu_done, 1)
                y_transposed(2 + l * 4, br_f)

                act.wait_ge(section, end + END_A)
                columns(base + L_B, 4, section_of)
                act.wait_ge(evac_act, evac0 + 9)
                act.activation(flat(U[:, 3, :, :]), flat(U[:, 3, :, :]), ACT.Silu).then_inc(silu_done, 1)
                heads_T(tb0 + 4, (0, 1), QK2[:, 0, :, :])
                heads_T(tb0 + 6, (2, 3), QK2[:, 1, :, :])
                head_std(HN0 + l * HN + 1, 8)
                y_transposed(2 + l * 4 + 1, br_f, gain=LV("ret_g"))

                act.wait_ge(section, end + END_B)
                columns(base + L_C, 4, section_of)
                act.wait_ge(evac_act, evac0 + 13)
                act.activation(flat(U[:, 3, :, :]), flat(U[:, 3, :, :]), ACT.Silu).then_inc(silu_done, 1)
                for q in range(2):
                    act.wait_ge(T_ps, tb0 + 8 + q + 1)
                    act.activation(flat(T[1][:, 2 * q:2 * q + 2, :]), pm[q][:, :], ACT.Sigmoid).then_inc(T_sb, 1)
                heads_T(tb0 + 10, (2, 3), T[2])
                head_std(HN0 + l * HN + 2, 8)
                y_transposed(2 + l * 4 + 2, br_f, gain=LV("hgrn_g"))

                act.wait_ge(section, end + END_C)
                columns(base + L_M, 2, section_of)
                act.wait_ge(evac_act, evac0 + 15)
                act.activation(flat(U[:, 1, :, :]), flat(U[:, 1, :, :]), ACT.Silu).then_inc(silu_done, 1)
                head_std(HN0 + l * HN + 3, 8)
                heads_T(tb0 + 12, (0, 1), QK2[:, 0, :, :], scale=gq[:, 1:2])
                attn(AT0 + l * AT + 1, sections_as_scores(8), view(24, NH, TB, S))
                y_transposed(2 + l * 4 + 3, br_f)

                act.wait_ge(section, end + END_M)
                with act.Fori(0, NB) as n:
                    for i in range(4):
                        g = base + L_G + n * 5 + i
                        advance(g)
                        if i == 0:
                            act.wait_ge(evac_dve, V_L + l * V_PER + n * 4)
                        take(g, i % 2, flat(sg[:, i, :, :]), ACT.Sigmoid)
                    advance(base + L_G + n * 5 + 4)
                transposed(2 + l * 2 + 1, hf_m)
                with act.Fori(0, NB) as n:
                    advance(base + L_O + n)

        @block.tensor
        def _(pe):
            def passes(out, lhs, k, tb, slot, c, start, stop):
                hi, lo = (v[:, k, tb * P:(tb + 1) * P] for v in lhs)
                pe.matmul(out, hi, w_hi[:, slot, c, :], start=start, stop=False)
                pe.matmul(out, hi, w_lo[:, slot, c, :], start=False, stop=False)
                return pe.matmul(out, lo, w_hi[:, slot, c, :], start=False, stop=stop)

            def group(G, b, lhs):
                for g in range(GT):
                    pe.wait_ge(lo_done, G * GT + g + 1)
                    for c in range(KC):
                        k = g * KC + c
                        for tb in range(TB):
                            i = passes(pg[b][:, tb, :], lhs, k, tb, g % RING, c, k == 0, k == KD - 1)
                    i.then_inc(tile_used, 1)

            def short(G, n, lhs):
                for g in (2 * n, 2 * n + 1):
                    pe.wait_ge(lo_done, G * GT + g + 1)
                    for c in range(KC):
                        k = (g % 2) * KC + c
                        for tb in range(TB):
                            i = passes(pg[n % 2][:, tb, :], lhs, k, tb, g % RING, c, k == 0, k == 3)
                    i.then_inc(tile_used, 1)

            def columns(base, n, lhs, free, done, after=None):
                pe.sem_inc(waited, 1)
                with pe.Fori(0, n // 2) as j:
                    for i in range(2):
                        pe.wait_ge(free, done + j * 2 + i - 1)
                        group(base + j * 2 + i, i, lhs)
                    if after is not None:
                        after(j)
                if n % 2:
                    pe.wait_ge(free, done + n - 2)
                    group(base + n - 1, 0, lhs)

            hT = (hT_hi, hT_lo)

            def transposes(rows, banks, out_sem):
                for q, b in enumerate(banks):
                    for c in range(2):
                        for tb in range(TB):
                            i = pe.transpose(pm[b][:, c * S + tb * P:c * S + (tb + 1) * P],
                                             rows[:, tb, (2 * q + c) * P:(2 * q + c + 1) * P], ident)
                    i.then_inc(out_sem, 1)

            def rows_T(occ, rows):
                for q in range(GT):
                    if q == 0:
                        pe.wait_ge(rows_ready, occ + 1)
                    if q >= 4:
                        pe.wait_ge(hf_done, occ * GT + q - 3)
                    for c in range(KC):
                        k = q * KC + c
                        for tb in range(TB):
                            i = pe.transpose(pm[q % 4][:, c * S + tb * P:c * S + (tb + 1) * P],
                                             rows[:, tb, k * P:(k + 1) * P], ident)
                    i.then_inc(rowsT_ps, 1)

            def attn(occ, qT, kT, S_, PT, v, t_value, forget=None):
                pe.wait_ge(T_sb, t_value)
                for h in range(NH):
                    for tb in range(TB):
                        out = pm[h][:, tb * S:(tb + 1) * S]
                        i = pe.matmul(out, qT[:, h, tb * P:(tb + 1) * P], kT[:, h, :], start=True,
                                      stop=forget is None)
                        if forget is not None:
                            i = pe.matmul(out, row[0:8, forget + h, :], F_row[0:8, :], start=False, stop=True)
                    i.then_inc(logit_ps, 1)
                for h in range(NH):
                    pe.wait_ge(exp_done, occ * NH + h + 1)
                    for sb_ in range(TB):
                        for tb in range(TB):
                            i = pe.transpose(pm[h][:, sb_ * S + tb * P:sb_ * S + (tb + 1) * P],
                                             S_[:, h, tb, sb_ * P:(sb_ + 1) * P], ident)
                    i.then_inc(P_T_ps, 1)
                pe.wait_ge(P_T_sb, (occ + 1) * NH)
                outs(PT, v)

            def outs(PT, v, causal_=False):
                for tb in range(TB):
                    for h in range(NH):
                        blocks = range(tb + 1) if causal_ else range(TB)
                        for sb_ in blocks:
                            i = pe.matmul(pm[tb][:, h * P:(h + 1) * P], PT[:, h, sb_, tb * P:(tb + 1) * P],
                                          v[:, sb_, h * P:(h + 1) * P], start=(sb_ == 0),
                                          stop=(sb_ == blocks[-1]))
                    i.then_inc(o_ps, 1)

            def y_T(occ, rows):
                pe.wait_ge(y_ready, occ + 1)
                transposes(rows, (2, 3), y_T_ps)

            def ada_sums(q, after):
                pe.wait_ge(ada_used, ADA_RING + (q + 1) * KD)
                if after:
                    pe.wait_ge(mod_taken, q)
                for m in range(AQ // P):
                    i = pe.matmul(pm[0][:, m:m + 1], ada_acc[:, m * P:(m + 1) * P], ones[:, 0:1],
                                  start=True, stop=True)
                i.then_inc(mod_ps, 1)

            pe.wait_ge(consts_in, 48)
            pe.wait_ge(memT_ready, 1)
            for l in range(LAYERS):
                for i in range(2):
                    if l > 0:
                        pe.wait_ge(evac_act, 2 * l + i - 1)
                    group(G_MEM + 2 * l + i, i, hT)
                ada_sums(l, l > 0)
                pe.wait_ge(hn_ready, l + 1)
                transposes(mk_tok, (2, 3), T_ps)

            rows_T(0, xn_1)
            pe.wait_ge(lw_in, 16)
            pe.wait_ge(hT_ready, 1)
            for tb in range(TB):
                for k in range(KD):
                    i = pe.matmul(pm[0][:, tb * 8:(tb + 1) * 8], hf_1[:, k, tb * P:(tb + 1) * P], w_f[:, k, :],
                                  start=(k == 0), stop=(k == KD - 1))
            i.then_inc(zf_ps, 1)
            columns(G_IN, 9, hT, evac_act, A_IN, after=lambda j: ada_sums(j + 2, True))

            pe.wait_ge(cons1_in, 16 * 4)
            pe.wait_ge(logf_ready, 1)
            for sb_ in range(TB):
                pe.matmul(pm[0][0:8, 0:S], logf[:, sb_, :], tri[:, sb_, :], start=(sb_ == 0), stop=(sb_ == 1))
            for tb in range(TB):
                for sb_ in range(tb + 1):
                    i = pe.matmul(pm[0][:, S + tb * 8:S + (tb + 1) * 8], tri[:, sb_, tb * P:(tb + 1) * P],
                                  logf[:, sb_, :], start=(sb_ == 0), stop=(sb_ == tb))
            i.then_inc(F_ps, 1)
            pe.wait_ge(evac_act, A_IN + 9)
            for q in range(2):
                for c in range(2):
                    g = 2 * q + c
                    for sb_ in range(TB):
                        i = pe.matmul(pm[2 + q][:, c * S:(c + 1) * S], Z[:, 6, sb_, g * P:(g + 1) * P],
                                      band[:, sb_, g, :], start=(sb_ == 0), stop=(sb_ == 1))
                i.then_inc(pool_ps, 1)
            pe.wait_ge(F_sb, 2)
            for q in range(2):
                pe.wait_ge(pool_sb, q + 1)
                for c in range(2):
                    g = 2 * q + c
                    i = pe.matmul(pm[q][:, c * S:(c + 1) * S], pool_w[:, g, :], pool_d[:, g, :],
                                  start=True, stop=True)
                i.then_inc(pool_ps, 1)
            for b in range(2):
                if b == 0:
                    pe.wait_ge(pool_sb, 4)
                else:
                    pe.wait_ge(y_T_sb, 2)
                transposes(Z[:, 3 * b, :, :], (0, 1), T_ps)
                transposes(Z[:, 3 * b + 1, :, :], (2, 3), T_ps)
                attn(b, QK1[:, 0, :, :], QK1[:, 1, :, :], sections_as_scores(12 * b),
                     QK1.rearrange("p q h s -> p (q h s)").rearrange("p (h a s) -> p h a s", h=NH, a=TB),
                     Z[:, 3 * b + 2, :, :], 8 + 4 * b, forget=4 * b)
                y_T(b, o1)
            transposes(Z[:, 7, :, :], (0, 1), lru_ps)
            pe.wait_ge(y_T_sb, 4)
            transposes(Z[:, 8, :, :], (2, 3), lru_ps)
            pe.wait_ge(lru_dve, 2)
            for gate in range(2):
                pe.wait_ge(lru_act, 2 + 2 * gate)
                for b in range(4):
                    i = pe.matmul(pm[2 * gate + b // 2][:, (b % 2) * S:(b % 2 + 1) * S], lru_w[:, gate, b, :],
                                  X_[:, b, :], start=True, stop=True)
                i.then_inc(lru_ps, 1)

            def broadcast(occ, dg, wait):
                pe.wait_ge(bc_dg, occ + 1)
                wait()
                for n in range(NB):
                    pe.matmul(pm[n][:, :], ones, flat(dg[:, 4 * n:4 * n + 4, :]), start=True,
                              stop=True).then_inc(bc_ps, 1)

            broadcast(0, dg1, lambda: pe.wait_ge(lru_act, 6))
            pe.wait_ge(section, END_MIX)
            columns(G_OUT, NB, hT, evac_dve, V_OUT)
            rows_T(1, xn)
            broadcast(1, dg1, lambda: pe.wait_ge(hf_done, 2 * GT))

            def ff_T(j):
                pe.wait_ge(evac_act, A_FF + j * 2 + 2)
                transposes(g_tok, (0, 1), ff_ps)
                transposes(u_tok, (2, 3), ff_ps)

            def down(G, j, taken):
                pe.wait_ge(aT_ready, j + 1)
                for n in range(NB):
                    pe.wait_ge(evac_dve, V_FF + j * NB + n - 1)
                    pe.wait_ge(evac_act, taken - (1 if n == 0 else 0))
                    short(G, n, (aT_hi, aT_lo))

            pe.wait_ge(section, END_NORM2)
            group(G_FF, 0, hT)
            group(G_FF + 1, 1, hT)
            with pe.Fori(0, NFF - 1) as j:
                g0 = G_FF + 2 + j * 3
                pe.wait_ge(evac_act, A_FF + j * 2 + 1)
                pe.wait_ge(evac_dve, V_FF + j * NB - 1)
                group(g0, 0, hT)
                ff_T(j)
                pe.wait_ge(evac_dve, V_FF + j * NB)
                group(g0 + 1, 1, hT)
                down(g0 + 2, j, A_FF + j * 2 + 4)
            ff_T(NFF - 1)
            down(G_FF + 3 * NFF - 1, NFF - 1, A_FF + 2 * NFF)
            broadcast(2, dg3, lambda: pe.wait_ge(section, END_FF))

            with pe.Fori(0, LAYERS) as l:
                base = G_LAYER + l * PER_LAYER
                end = END_B1 + l * PER_END
                tb0 = 12 + l * 14
                evac0 = A_L + l * A_PER
                pe.wait_ge(section, end)
                rows_T(2 + l * 2, xn)
                pe.wait_ge(lw_in, 16 * (3 + 2 * l))
                pe.wait_ge(hT_ready, 3 + l * 2)
                for tb in range(TB):
                    for k in range(KD):
                        i = pe.matmul(pm[0][:, tb * SMALL:(tb + 1) * SMALL], hf[:, k, tb * P:(tb + 1) * P],
                                      small_w[:, k * SMALL:(k + 1) * SMALL], start=(k == 0), stop=(k == KD - 1))
                i.then_inc(small_ps, 1)

                columns(base, 5, hT, evac_act, evac0)
                pe.wait_ge(evac_act, evac0 + 5)
                pe.wait_ge(small_sb, l * 3 + 3)
                transposes(U[:, 4, :, :], (0, 1), idx_ps)
                for tb in range(TB):
                    i = pe.transpose(pm[2][:, tb * P:(tb + 1) * P], ki2[:, tb, :], ident)
                i.then_inc(idx_ps, 1)
                for h in range(IDX_HEADS):
                    if h == 0:
                        pe.wait_ge(idx_sb, l * 3 + 3)
                    if h >= 4:
                        pe.wait_ge(rel_sb, l * IDX_HEADS + h - 3)
                    half = slice((h % 2) * 64, (h % 2) * 64 + 64)
                    for tb in range(TB):
                        i = pe.matmul(pm[h % 4][:, tb * S:(tb + 1) * S], qiT[half, h // 2, tb * P:(tb + 1) * P],
                                      kiT[half, :], start=True, stop=True)
                    i.then_inc(rel_ps, 1)
                pe.wait_ge(rel_sb, (l + 1) * IDX_HEADS)
                pe.wait_ge(hn_ready, HN0 + l * 2 + 1)
                transposes(U[:, 0, :, :], (0, 1), T_ps)
                transposes(U[:, 1, :, :], (2, 3), T_ps)
                attn(AT0 + l * AT, QK2[:, 0, :, :], QK2[:, 1, :, :], sections_as_scores(0), view(20, NH, TB, S),
                     U[:, 2, :, :], tb0 + 4)
                y_T(2 + l * 4, U[:, 4, :, :])

                pe.wait_ge(section, end + END_A)
                columns(base + L_B, 4, hT, evac_act, evac0 + 5)
                pe.wait_ge(rope_done, l + 1)
                transposes(rows_b[:, 0, :, :], (0, 1), T_ps)
                transposes(rows_b[:, 1, :, :], (2, 3), T_ps)
                pe.wait_ge(T_sb, tb0 + 8)
                for h in range(NH):
                    pe.matmul(pm[h][:, 0:S], QK2[:, 1, h, 0:P], QK2[:, 0, h, :], start=True, stop=True)
                    pe.matmul(pm[h][:, S + P:], QK2[:, 1, h, P:], QK2[:, 0, h, P:], start=True,
                              stop=True).then_inc(ret_ps, 1)
                pe.wait_ge(ret_sb, (l + 1) * NH)
                outs(view(28, NH, TB, S), U[:, 2, :, :], causal_=True)
                y_T(2 + l * 4 + 1, U[:, 0, :, :])

                pe.wait_ge(section, end + END_B)
                columns(base + L_C, 4, hT, evac_act, evac0 + 9)
                pe.wait_ge(evac_act, evac0 + 13)
                transposes(U[:, 0, :, :], (0, 1), T_ps)
                transposes(U[:, 2, :, :], (2, 3), T_ps)
                for r in range(SUB):
                    pe.wait_ge(W_ready, l * SUB + r + 1)
                    w = flat((T[6], T2)[r % 2])
                    for hp in range(2):
                        i = pe.matmul(pg[0][:, hp, :], sel[:, SUB - r:SUB - r + P], w[:, hp * NW:(hp + 1) * NW],
                                      start=(r == 0), stop=(r == SUB - 1))
                    i.then_inc(W_used, 1)
                for i in range(1, NSUB):
                    pe.wait_ge(K_ready, l * (NSUB - 1) + i)
                    K = (T[0], T[1])[i % 2]
                    for h in range(NH):
                        for sb_ in range(1 if i * SUB <= P else 2):
                            j = pe.matmul(pm[h][:, sb_ * S + i * SUB:sb_ * S + (i + 1) * SUB],
                                          K[:, h, sb_ * P:(sb_ + 1) * P], T[3][:, h, i * SUB:(i + 1) * SUB],
                                          start=True, stop=True)
                    j.then_inc(A_ps, 1)
                pe.wait_ge(A_sb, l + 1)
                outs(view(32, NH, TB, S), U[:, 1, :, :], causal_=True)
                y_T(2 + l * 4 + 2, T[2].rearrange("p h s -> p (h s)").rearrange("p (a n) -> p a n", a=TB))

                pe.wait_ge(section, end + END_C)
                columns(base + L_M, 2, hT, evac_act, evac0 + 13)
                pe.wait_ge(hn_ready, HN0 + l * 2 + 2)
                transposes(U[:, 0, :, :], (0, 1), T_ps)
                attn(AT0 + l * AT + 1, QK2[:, 0, :, :],
                     mk_T[:, bass.ds(l, 1), :, :].rearrange("p o h s -> p (o h) s"), sections_as_scores(8),
                     view(24, NH, TB, S), mv[:, bass.ds(l, 1), :, :].rearrange("p o a n -> p (o a) n"), tb0 + 14)
                y_T(2 + l * 4 + 3, U[:, 0, :, :])

                pe.wait_ge(section, end + END_M)
                pe.sem_inc(waited, 1)
                with pe.Fori(0, NB) as n:
                    for i in range(4):
                        pe.wait_ge(evac_dve, V_L + l * V_PER + n * 4 - (1 if i == 0 else 0))
                        pe.wait_ge(evac_act, evac0 + IN2 + n * 4 + i - 1)
                        group(base + L_G + n * 5 + i, i % 2, hT)
                    for i in range(4):
                        pe.wait_ge(evac_act, evac0 + IN2 + n * 4 + min(i + 3, 4))
                        pe.wait_ge(evac_dve, V_L + l * V_PER + n * 4 + i - 1)
                        short(base + L_G + n * 5 + 4, i, (yT_hi[:, i, :, :], yT_lo[:, i, :, :]))
                rows_T(2 + l * 2 + 1, merged)
                pe.wait_ge(hT_ready, 2 + l * 2 + 2)
                columns(base + L_O, NB, hT, evac_dve, V_L + l * V_PER + 16)

        @block.vector
        def _(dve):
            step = Steps(dve, dve_step)
            tt, stt, ts = dve.tensor_tensor, dve.scalar_tensor_tensor, dve.tensor_scalar

            def split(group, tiles):
                for g in tiles:
                    dve.wait_ge(hi_done, group * GT + g + 1)
                    tt(flat(w_lo[:, g % RING, :, :]), raw[:, g % RING, :],
                       flat(w_hi[:, g % RING, :, :]).bitcast(F32), ALU.subtract).then_inc(lo_done, 1)

            def advance(group, weigh=None):
                for i in range(GT):
                    split(group + (i >= 4), ((i + 4) % GT,))
                    if weigh is not None:
                        weigh(i)

            def columns(base, n):
                dve.sem_inc(waited, 1)
                with dve.Fori(0, n) as j:
                    advance(base + j)

            def split_act(src, hi, lo, sem_):
                step(dve.tensor_copy(hi, src))
                step.settle()
                tt(lo, src, hi.bitcast(F32), ALU.subtract).then_inc(sem_, 1)

            def end_section():
                step.settle()
                dve.sem_inc(section, 1)

            def row_norm(occ):
                dve.wait_ge(ssq_done, 2 * occ + 2)
                ts(ssq, ssq, 1.0 / D, EPS, ALU.mult, ALU.add).then_inc(var_done, 1)
                dve.wait_ge(std_done, occ + 1)
                step(dve.reciprocal(rstd, rstd))
                step.settle()

            def norm(occ, occ_t, xn=xn, hf=hf):
                row_norm(occ)
                step(ts(xn[:, 0, :], x[:, 0, :], rstd[:, 0:1], None, ALU.mult))
                step.settle()
                ts(xn[:, 1, :], x[:, 1, :], rstd[:, 1:2], None, ALU.mult).then_inc(rows_ready, 1)
                split_T(occ_t, hf)

            def split_T(occ_t, src):
                for q in range(4):
                    dve.wait_ge(hf_done, occ_t * GT + 2 * q + 2)
                    a = slice(4 * q, 4 * q + 4)
                    step(dve.tensor_copy(hT_hi[:, a, :], src[:, a, :]))
                    step.settle()
                    i = tt(hT_lo[:, a, :], src[:, a, :], hT_hi[:, a, :].bitcast(F32), ALU.subtract)
                    if q < 3:
                        step(i)
                    else:
                        i.then_inc(hT_ready, 1)

            def head_squares(src, sq, at, n):
                step(tt(sq, src, src, ALU.mult))
                step.settle()
                step(dve.tensor_reduce(hss[:, at:at + n], sq.rearrange("p (n d) -> p n d", d=HD), AX.X, ALU.add))
                step.settle()

            def head_std(occ, n):
                ts(hss[:, 0:n], hss[:, 0:n], 1.0 / HD, EPS, ALU.mult, ALU.add).then_inc(hss_done, 1)
                dve.wait_ge(hstd_done, occ + 1)
                step(dve.reciprocal(hrs[:, 0:n], hrs[:, 0:n]))
                step.settle()

            def by_head(out, src, scal, n, sem_=None):
                v = lambda a: a.rearrange("p (n d) -> p n d", d=HD)
                i = tt(v(out), v(src), scal.unsqueeze(2).to_broadcast([P, n, HD]), ALU.mult)
                if sem_ is None:
                    step(i)
                    step.settle()
                else:
                    i.then_inc(sem_, 1)

            def attn(occ, S_, mask, forget=None):
                for h in range(NH):
                    dve.wait_ge(logit_ps, occ * NH + h + 1)
                    for tb in range(TB):
                        src = pm[h][:, tb * S:(tb + 1) * S]
                        if forget is not None:
                            step(stt(S_[:, h, tb, :], src, F_t[:, tb, forget + h:forget + h + 1],
                                     mask[:, tb, :], ALU.add, ALU.add))
                        elif mask is not None:
                            step(tt(S_[:, h, tb, :], src, mask[:, tb, :], ALU.add))
                        else:
                            step(dve.tensor_copy(S_[:, h, tb, :], src))
                    step.settle()
                    dve.tensor_reduce(nmax[:, 2 * h:2 * h + 2], S_[:, h, :, :], AX.X, ALU.max,
                                      negate=True).then_inc(max_done, 1)
                dve.wait_ge(exp_done, (occ + 1) * NH)
                step(dve.reciprocal(rsum, psum_of))
                step.settle()

            def attn_out(o_value, o, final=None):
                for tb in range(TB):
                    dve.wait_ge(o_ps, o_value + tb + 1)
                    scal = rsum.rearrange("p (h a) -> p a h", a=TB)[:, tb, :]
                    last = tb == 1 and final is not None
                    by_head(o[:, tb, :], pm[tb][:, :], scal, NH, final if last else None)

            def branch_out(l, n, o, z):
                dve.wait_ge(silu_done, l * 4 + n + 1)
                tt(flat(o), flat(o), flat(z), ALU.mult).then_inc(y_ready, 1)
                dve.wait_ge(y_T_sb, 4 + (l * 4 + n + 1) * 2)
                split_act(br_f, yT_hi[:, n, :, :], yT_lo[:, n, :, :], section)

            dve.sem_inc(evac_dve, 2)
            dve.sem_inc(W_used, 2)

            def weigh(q, k):
                dve.wait_ge(ada_in[k % ADA_RING], (q * (KD // ADA_RING) + k // ADA_RING + 1) * 16)
                dve.wait_ge(ada_used, ADA_RING + q * KD + k)
                chunk = ada_ring[:, k % ADA_RING, :]
                if k == 0:
                    i = ts(ada_acc, chunk, c_act[:, 0:1], None, ALU.mult)
                else:
                    i = stt(ada_acc, chunk, c_act[:, k:k + 1], ada_acc, ALU.mult, ALU.add)
                i.then_inc(ada_used, 1)

            def take_mod(q):
                dve.wait_ge(mod_ps, q + 1)
                tt(mod[:, bass.ds(q * KD, KD)], pm[0][:, 0:KD], vec[:, bass.ds(VEC["b_ada"][0] + q * KD, KD)],
                   ALU.add).then_inc(mod_taken, 1)

            dve.sem_inc(ada_used, ADA_RING)
            dve.wait_ge(c_ready, 1)
            L0, L1 = V("lb")[:, 0:4], V("lb")[:, 4:8]
            step(tt(t8[:, 0:4], L0, L1, ALU.max))
            step.settle()
            step(tt(t8[:, 4:8], L0, t8[:, 0:4], ALU.subtract))
            step(tt(t8[:, 8:12], L1, t8[:, 0:4], ALU.subtract))
            step.settle()
            step(ts(t8[:, 12:16], V("lam"), -1.0, None, ALU.mult))
            step.settle()
            tt(spl[:, 4:8], V("lam"), t8[:, 12:16], ALU.min).then_inc(lam_in, 1)
            step(ts(t8[:, 12:16], t8[:, 12:16], 0.0, None, ALU.max))

            dve.wait_ge(mem_in, 16)
            step(dve.tensor_copy(flat(hT_hi[:, :, :]), flat(mem_f)))
            step.settle()
            tt(flat(hT_lo[:, :, :]), flat(mem_f), flat(hT_hi[:, :, :]).bitcast(F32), ALU.subtract
               ).then_inc(memT_ready, 1)
            split(0, range(4))
            for l in range(LAYERS):
                for i in range(2):
                    advance(G_MEM + 2 * l + i, lambda k: weigh(l, i * GT + k))
                take_mod(l)
                dve.wait_ge(evac_act, 2 * l + 1)
                head_squares(flat(mk_tok), flat(mk_sq), 0, 8)
                head_std(l, 8)
                by_head(flat(mk_tok), flat(mk_tok), hrs[:, 0:8], 8, hn_ready)
                dve.wait_ge(T_sb, 2 * l + 2)
                end_section()
                dve.wait_ge(section, END_MEM0 + l)

            dve.wait_ge(mod_taken, 2)
            step(ts(mod[:, 16:32], mod[:, 16:32], 1.0, None, ALU.add))
            step.settle()
            step(tt(mod[:, 16:32], mod[:, 16:32], V("g_mix"), ALU.mult))
            end_section()
            dve.wait_ge(x_in, 16)
            norm(0, 0, xn_1, hf_1)
            dve.wait_ge(lam_out, 3)
            step(tt(spl[:, 0:4], spl[:, 0:4], t8[:, 12:16], ALU.add))
            step.settle()
            step(ts(spl[:, 0:4], spl[:, 0:4], -8.0, None, ALU.mult))
            step(tt(t8[:, 0:4], t8[:, 4:8], t8[:, 8:12], ALU.add))
            step.settle()
            step(dve.reciprocal(t8[:, 0:4], t8[:, 0:4]))
            step.settle()
            step(tt(t8[:, 4:8], t8[:, 4:8], t8[:, 0:4], ALU.mult))
            step(tt(t8[:, 8:12], t8[:, 8:12], t8[:, 0:4], ALU.mult))
            step.settle()
            step(tt(lb[:, 0:4], t8[:, 4:8], t8[:, 4:8], ALU.subtract))
            step(tt(lb[:, 4:8], t8[:, 4:8], t8[:, 8:12], ALU.add))
            step.settle()
            step(tt(lb[:, 4:8], lb[:, 4:8], t8[:, 4:8], ALU.subtract))
            dve.wait_ge(consts_in, 48)
            dve.wait_ge(zf_ps, 1)
            step(tt(zf, pm[0][:, 0:TB * 8].rearrange("p (a h) -> p a h", a=TB),
                    b_f.unsqueeze(1).to_broadcast([P, TB, 8]), ALU.add))
            step.settle()
            step(ts(flat(F_t), flat(zf), -1.0, None, ALU.mult))
            step.settle()
            tt(flat(logf), flat(zf), flat(F_t), ALU.min).then_inc(zf_in, 1)
            end_section()
            dve.sem_inc(waited, 1)
            with dve.Fori(0, 4) as j:
                for i in range(2):
                    advance(G_IN + j * 2 + i, lambda k: weigh(j + 2, i * GT + k))
                take_mod(j + 2)
            advance(G_IN + 8)
            dve.wait_ge(mod_taken, NQ)
            step(ts(mod[:, 64:80], mod[:, 64:80], 1.0, None, ALU.add))
            step.settle()
            step(tt(mod[:, 64:80], mod[:, 64:80], V("g_ffn"), ALU.mult))
            dve.wait_ge(zf_out, 2)
            stt(flat(logf), flat(zf), 0.0, flat(logf), ALU.min, ALU.subtract).then_inc(logf_ready, 1)
            dve.wait_ge(F_sb, 2)
            for b in range(2):
                attn(b, sections_as_scores(12 * b), causal, forget=4 * b)
                attn_out(2 * b, o1, final=y_ready)
            dve.wait_ge(evac_act, A_IN + 9)
            dve.wait_ge(y_T_sb, 4)
            dve.sem_inc(lru_dve, 1)
            dve.wait_ge(lru_act, 2)
            for k in (2, 1, 0):
                d = 3 - k
                for b in range(4):
                    src = pm[b // 2][:, (b % 2) * S:(b % 2 + 1) * S]
                    step(stt(X_[:, b, d:], src[:, 0:S - d], V("conv_w")[:, 4 * b + k:4 * b + k + 1],
                             X_[:, b, d:], ALU.mult, ALU.add))
                step.settle()
            dve.sem_inc(lru_dve, 1)
            dve.wait_ge(lru_act, 5)
            for b in range(4):
                step(ts(GR[:, b, :], GR[:, b, :], spl[:, b:b + 1], None, ALU.mult))
            step.settle()
            dve.sem_inc(lru_dve, 1)
            dve.wait_ge(lru_act, 6)
            step(tt(flat(GI), flat(GI), flat(X_), ALU.mult))
            dve.wait_ge(lru_act, 8)
            step(tt(flat(GR), flat(Y_), flat(Y_), ALU.mult))
            step.settle()
            step(ts(flat(GR), flat(GR), 0.044715, 1.0, ALU.mult, ALU.add))
            step(tt(flat(X_), flat(A_), flat(A_), ALU.mult))
            step.settle()
            stt(flat(TH), flat(X_), 1.0, flat(TH), ALU.add, ALU.mult).then_inc(lru_dve, 1)
            tt(flat(GR), flat(GR), flat(Y_), ALU.mult).then_inc(lru_dve, 1)
            dve.wait_ge(lru_act, 9)
            step(tt(flat(GI), flat(GI), flat(TH), ALU.mult))
            step.settle()
            for b in range(4):
                step(dve.tensor_tensor_scan(X_[:, b, :], A_[:, b, :], GI[:, b, :], 0.0, ALU.mult, ALU.add))
            dve.wait_ge(lru_act, 10)
            step(stt(flat(GR), flat(GR), 1.0, flat(Y_), ALU.add, ALU.mult))
            step.settle()
            step(stt(flat(YT[:, 12:16, :]), flat(GR), 0.5, flat(X_), ALU.mult, ALU.mult))
            dve.wait_ge(pool_sb, 4)
            step.settle()
            step(dve.tensor_copy(hT_hi[:, :, :], YT))
            step.settle()
            step(tt(hT_lo[:, :, :], YT, hT_hi[:, :, :].bitcast(F32), ALU.subtract))

            def diagonal(dg, v):
                tt(dg, ident.unsqueeze(1).to_broadcast([P, KD, P]), v.unsqueeze(2).to_broadcast([P, KD, P]),
                   ALU.mult).then_inc(bc_dg, 1)

            step.settle()
            diagonal(dg1, mod[:, 32:48])
            dve.wait_ge(bc_done, NB)
            end_section()

            def residual(G, b, n, gated):
                dve.wait_ge(tile_used, (G + 1) * GT)
                xs = x[:, :, bass.ds(n * NW, NW)]
                if gated:
                    gb = gate_b[:, bass.ds(n * NW, NW)].unsqueeze(1).to_broadcast([P, TB, NW])
                    step(tt(o_tmp, pg[b][:, :, :], gb, ALU.mult))
                    step.settle()
                    tt(xs, xs, o_tmp, ALU.add).then_inc(evac_dve, 1)
                else:
                    tt(xs, xs, pg[b][:, :, :], ALU.add).then_inc(evac_dve, 1)

            with dve.Fori(0, NB // 2) as j:
                step.enter(j, 2)
                for i in range(2):
                    advance(G_OUT + j * 2 + i)
                    residual(G_OUT + j * 2 + i, i, j * 2 + i, True)
                    dve.wait_ge(evac_dve, V_OUT + j * 2 + i + 1)
                step.leave(NB // 2, 2)
            end_section()
            norm(1, 1)
            diagonal(dg1, mod[:, 80:96])
            dve.wait_ge(bc_done, 2 * NB)
            dve.wait_ge(hT_ready, 2)
            step(dve.memset(flat(F_acc), 0.0))
            step.settle()
            end_section()

            def conv(j):
                dve.wait_ge(ff_tap, 2 * j + 2)
                for k in (1, 0):
                    d = 2 - k
                    for m in range(4):
                        src = pm[m // 2][:, (m % 2) * S:(m % 2 + 1) * S]
                        w = vec[:, bass.ds(VEC["ffn_w"][0] + (j * 4 + m) * 3 + k, 1)]
                        step(stt(g_cv[:, m, d:], src[:, 0:S - d], w, g_cv[:, m, d:], ALU.mult, ALU.add))
                    step.settle()
                dve.sem_inc(ff_conv, 1)

            def product(j):
                dve.wait_ge(ff_silu, j + 1)
                dve.wait_ge(ff_ps, j * 4 + 4)
                for q in range(2):
                    step(tt(flat(a_f[:, 2 * q:2 * q + 2, :]), flat(g_cv[:, 2 * q:2 * q + 2, :]), pm[2 + q][:, :],
                            ALU.mult))
                step.settle()
                split_act(a_f, aT_hi, aT_lo, aT_ready)

            def down_out(G, j, n):
                dve.wait_ge(tile_used, G * GT + 2 * n + 2)
                F_ = F_acc[:, n, :, :]
                dve.wait_ge(evac_dve, V_FF + j * NB + n)
                tt(F_, F_, pg[n % 2][:, :, :], ALU.add).then_inc(evac_dve, 1)

            advance(G_FF)
            advance(G_FF + 1)
            with dve.Fori(0, NFF - 1) as j:
                step.enter(j, 11)
                g0 = G_FF + 2 + j * 3
                advance(g0)
                conv(j)
                split(g0 + 1, range(4, 6))
                product(j)
                split(g0 + 1, range(6, 8))
                split(g0 + 2, range(6))
                down_out(g0 + 2, j, 0)
                split(g0 + 2, range(6, 8))
                down_out(g0 + 2, j, 1)
                split(g0 + 3, range(2))
                down_out(g0 + 2, j, 2)
                split(g0 + 3, range(2, 4))
                down_out(g0 + 2, j, 3)
                step.leave(NFF - 1, 11)
            conv(NFF - 1)
            product(NFF - 1)
            GL = G_FF + 3 * NFF - 1
            split(GL, range(4, 6))
            down_out(GL, NFF - 1, 0)
            split(GL, range(6, 8))
            down_out(GL, NFF - 1, 1)
            split(GL + 1, range(2))
            down_out(GL, NFF - 1, 2)
            split(GL + 1, range(2, 4))
            down_out(GL, NFF - 1, 3)
            dve.wait_ge(evac_dve, V_L)
            step(tt(F_acc, F_acc, gate_b.rearrange("p (n c) -> p n c", n=NB).unsqueeze(2)
                    .to_broadcast([P, NB, TB, NW]), ALU.mult))
            step.settle()
            xv = x[:, :, :].rearrange("p a (n c) -> p n a c", n=NB)
            tt(xv, xv, F_acc, ALU.add).then_inc(section, 1)
            dve.wait_ge(section, END_FF)
            diagonal(dg3, V("final_g"))
            row_norm(2)
            dve.wait_ge(bc_done, 3 * NB)
            step(stt(x[:, 0, :], x[:, 0, :], rstd[:, 0:1], gate_b, ALU.mult, ALU.mult))
            step.settle()
            stt(x[:, 1, :], x[:, 1, :], rstd[:, 1:2], gate_b, ALU.mult, ALU.mult).then_inc(section, 1)


            with dve.Fori(0, LAYERS) as l:
                step.enter(l, LAYER_STEPS)
                base = G_LAYER + l * PER_LAYER
                evac0 = A_L + l * A_PER
                v0 = V_L + l * V_PER
                norm(3 + l, 2 + l * 2)
                dve.wait_ge(lw_in, 16 * (3 + 2 * l))
                step(ts(gq[:, 0:1], LV("qk_g")[:, 0:1], SCALE, None, ALU.mult))
                step(ts(gq[:, 1:2], LV("qk_g")[:, 2:3], SCALE, None, ALU.mult))
                step(dve.tensor_copy(lbc, sc[:, bass.ds(84 + l * NH, NH)]))
                step.settle()
                step(ts(oml, lbc, -1.0, 1.0, ALU.mult, ALU.add))
                dve.wait_ge(small_sb, l * 3 + 1)
                step(ts(wi.rearrange("p (a h) -> p a h", a=TB), small_u[:, :, IDX_DIM:], float(IDX_HEADS) ** -0.5,
                        None, ALU.mult))
                for i in range(2):
                    dve.tensor_copy(ki2[:, :, i * 64:(i + 1) * 64], small_u[:, :, 0:IDX_DIM]).then_inc(small_sb, 1)
                end_section()

                columns(base, 5)
                dve.wait_ge(evac_act, evac0 + 5)
                sq = view(20, TB, NW)
                head_squares(flat(U[:, 0, :, :]), flat(sq), 0, 8)
                head_squares(flat(U[:, 1, :, :]), flat(sq), 8, 8)
                head_std(HN0 + l * HN, 16)
                by_head(flat(U[:, 0:2, :, :]), flat(U[:, 0:2, :, :]), hrs, 16, hn_ready)
                for h in range(IDX_HEADS):
                    dve.wait_ge(rel_sb, l * IDX_HEADS + h + 1)
                    if h:
                        step.settle()
                        dve.wait_ge(rel_used, l * IDX_HEADS + h)
                    for tb in range(TB):
                        w = wi[:, tb * IDX_HEADS + h:tb * IDX_HEADS + h + 1]
                        if h == 0:
                            i = ts(score[:, tb, :], rel[:, h % 2, tb, :], w, None, ALU.mult)
                        else:
                            i = stt(score[:, tb, :], rel[:, h % 2, tb, :], w, score[:, tb, :], ALU.mult, ALU.add)
                        if tb == 0:
                            step(i)
                        else:
                            i.then_inc(rel_used, 1)
                step.settle()
                dve.wait_ge(rel_used, (l + 1) * IDX_HEADS)
                step(tt(score, score, visible, ALU.add))
                step.settle()
                for r in range(ROUNDS):
                    dve.sem_inc(waited, 1)
                    for tb in range(TB):
                        step(dve.max(top8[:, tb * 8:tb * 8 + 8], score[:, tb, :]))
                    step.settle()
                    dve.sem_inc(waited, 1)
                    for tb in range(TB):
                        step(dve.match_replace(score[:, tb, :], top8[:, tb * 8:tb * 8 + 8], score[:, tb, :], TAKEN))
                    step.settle()
                step(ts(score, score, (TAKEN + HIDDEN) / 2, FAR, ALU.is_gt, ALU.mult))
                step.settle()
                attn(AT0 + l * AT, sections_as_scores(0), score)
                attn_out(4 + l * 8, U[:, 4, :, :])
                branch_out(l, 0, U[:, 4, :, :], U[:, 3, :, :])

                columns(base + L_B, 4)
                dve.wait_ge(evac_act, evac0 + 9)
                for tb in range(TB):
                    heads = lambda v: v.rearrange("p s (h d) -> p s h d", d=HD)
                    u, r = heads(U[:, 0:2, tb, :]), heads(rows_b[:, :, tb, :])
                    a, b_ = (rope_t[:, i, :].rearrange("p (s h d) -> p s h d", s=2, h=NH) for i in range(2))
                    c_, s_ = (v[:, tb, :].unsqueeze(1).unsqueeze(1).to_broadcast([P, 2, NH, 64])
                              for v in (cos, sin))
                    t1, t2 = u[:, :, :, 0:64], u[:, :, :, 64:]
                    step(tt(r[:, :, :, 0:64], t1, c_, ALU.mult))
                    step(tt(a, t2, s_, ALU.mult))
                    step(tt(r[:, :, :, 64:], t1, s_, ALU.mult))
                    step(tt(b_, t2, c_, ALU.mult))
                    step.settle()
                    step(tt(r[:, :, :, 0:64], r[:, :, :, 0:64], a, ALU.subtract))
                    if tb:
                        step.settle()
                    i = tt(r[:, :, :, 64:], r[:, :, :, 64:], b_, ALU.add)
                    if tb == 0:
                        step(i)
                        step.settle()
                    else:
                        i.then_inc(rope_done, 1)
                PT = view(28, NH, TB, S)
                for h in range(NH):
                    dve.wait_ge(ret_ps, l * NH + h + 1)
                    step(tt(PT[:, h, 0, :].rearrange("p (a t) -> p a t", a=2),
                            pm[h][:, 0:S].rearrange("p (a t) -> p a t", a=2), decay[:, :, h, :], ALU.mult))
                step.settle()
                for h in range(NH):
                    tt(PT[:, h, 1, P:], pm[h][:, S + P:], decay[:, 0, h, :], ALU.mult).then_inc(ret_sb, 1)

                def normed_rows(n, o, sq_):
                    for tb in range(TB):
                        dve.wait_ge(o_ps, 4 + l * 8 + 2 * n + tb + 1)
                        step(dve.tensor_copy(o[:, tb, :], pm[tb][:, :]))
                    step.settle()
                    head_squares(flat(o), sq_, 0, 8)
                    head_std(HN0 + l * HN + n, 8)
                    by_head(flat(o), flat(o), hrs[:, 0:8], 8)

                normed_rows(1, U[:, 0, :, :], flat(rope_t))
                branch_out(l, 1, U[:, 0, :, :], U[:, 3, :, :])

                columns(base + L_C, 4)
                dve.wait_ge(evac_act, evac0 + 13)
                subs = lambda v: flat(v).rearrange("p (b r) -> p b r", r=SUB)
                dve.wait_ge(T_sb, 12 + l * 14 + 12)
                for h in range(NH):
                    step(ts(T[1][:, h, :], T[1][:, h, :], oml[:, h:h + 1], lbc[:, h:h + 1], ALU.mult, ALU.add))
                step(dve.memset(flat(T[4]), 0.0))
                step.settle()
                step(ts(flat(T[0]), flat(T[1]), -1.0, 1.0, ALU.mult, ALU.add))
                step(dve.tensor_copy(subs(T[4])[:, :, 0:1], subs(T[1])[:, :, 0:1]))
                step.settle()
                step(dve.memset(subs(T[1])[:, :, 0:1], 0.0))
                step.settle()
                step(dve.tensor_tensor_scan(flat(T[5]), flat(T[1]), flat(T[4]), 0.0, ALU.mult, ALU.add))
                step.settle()
                step(tt(flat(T[3]), flat(T[2]), flat(T[5]), ALU.mult))
                step(dve.tensor_copy(F_end.unsqueeze(2), subs(T[5])[:, :, SUB - 1:SUB]))
                step(dve.memset(subs(T[4])[:, :, 0:1], 0.0))
                step.settle()
                for r in range(SUB):
                    W = (T[6], T2)[r % 2]
                    step(dve.tensor_copy(subs(T[4])[:, :, r:r + 1], subs(T[0])[:, :, r:r + 1]))
                    step.settle()
                    step(dve.tensor_tensor_scan(flat(T[5]), flat(T[1]), flat(T[4]), 0.0, ALU.mult, ALU.add))
                    step.settle()
                    step(dve.memset(subs(T[4])[:, :, r:r + 1], 0.0))
                    step(dve.tensor_copy(subs(T0)[:, :, r:r + 1], subs(T[5])[:, :, SUB - 1:SUB]))
                    dve.wait_ge(W_used, l * SUB + r + 1)
                    tt(flat(W), flat(T[5]), flat(T[2]), ALU.mult).then_inc(W_ready, 1)
                    dve.wait_ge(W_ready, l * SUB + r + 1)
                    step.settle()
                for v in (T[0], T[1], T[4], T[5]):
                    step(dve.memset(flat(v), 0.0))
                step.settle()
                ends = F_end.rearrange("p (h b) -> p h b", h=NH)
                for i in range(1, NSUB):
                    K, before = (T[0], T[1])[i % 2], (T[0], T[1])[(i + 1) % 2]
                    n = (i - 1) * SUB
                    if i > 2:
                        dve.wait_ge(A_ps, l * (NSUB - 1) + i - 2)
                    new = dve.tensor_copy(K[:, :, n:n + SUB], T0[:, :, n:n + SUB])
                    if i == 1:
                        new.then_inc(K_ready, 1)
                    else:
                        step(new)
                        step.settle()
                        dve.wait_ge(K_ready, l * (NSUB - 1) + i - 1)
                        tt(K[:, :, 0:n], before[:, :, 0:n], ends[:, :, i - 1:i].to_broadcast([P, NH, n]),
                           ALU.mult).then_inc(K_ready, 1)
                A = view(32, NH, TB, S)
                dve.wait_ge(A_ps, (l + 1) * (NSUB - 1))
                for h in range(NH):
                    step(dve.tensor_copy(A[:, h, 0, SUB:], pm[h][:, SUB:S]))
                    step(dve.tensor_copy(A[:, h, 1, P + SUB:], pm[h][:, S + P + SUB:]))
                dve.wait_ge(W_used, (l + 1) * SUB + 2)
                tmp = T2[:, :, 0:S].rearrange("p h (a t) -> p a h t", a=TB)
                inside = pg[0][:, :, :].rearrange("p q (g a t) -> p a (q g) t", g=2, a=TB)
                for a in range(TB):
                    step(tt(tmp[:, a, :, :], inside[:, a, :, :], same.unsqueeze(1).to_broadcast([P, NH, P]),
                            ALU.mult))
                step.settle()
                for a in range(TB):
                    d = A[:, :, a, a * P:(a + 1) * P]
                    i = tt(d, d, tmp[:, a, :, :], ALU.add)
                    if a == 0:
                        step(i)
                        step.settle()
                i.then_inc(A_sb, 1)
                o_c = flat(T[2]).rearrange("p (a n) -> p a n", a=TB)
                normed_rows(2, o_c, flat(T[6]))
                branch_out(l, 2, o_c, U[:, 3, :, :])

                columns(base + L_M, 2)
                dve.wait_ge(evac_act, evac0 + 15)
                head_squares(flat(U[:, 0, :, :]), flat(rope_t), 0, 8)
                head_std(HN0 + l * HN + 3, 8)
                by_head(flat(U[:, 0, :, :]), flat(U[:, 0, :, :]), hrs[:, 0:8], 8, hn_ready)
                attn(AT0 + l * AT + 1, sections_as_scores(8), None)
                attn_out(4 + l * 8 + 6, U[:, 0, :, :])
                branch_out(l, 3, U[:, 0, :, :], U[:, 1, :, :])

                with dve.Fori(0, NB) as n:
                    step.enter(n, 3)
                    for i in range(4):
                        advance(base + L_G + n * 5 + i)
                    G = base + L_G + n * 5 + 4
                    for i, (group_, tiles_) in enumerate(((G, (4, 5)), (G, (6, 7)), (G + 1, (0, 1)), (G + 1, (2, 3)))):
                        split(group_, tiles_)
                        dve.wait_ge(tile_used, G * GT + 2 * i + 2)
                        dve.wait_ge(evac_act, evac0 + IN2 + n * 4 + i + 1)
                        m = merged[:, :, bass.ds(n * NW, NW)]
                        if i == 0:
                            tt(m, pg[0][:, :, :], sg[:, i, :, :], ALU.mult).then_inc(evac_dve, 1)
                        else:
                            step(tt(m_tmp, pg[i % 2][:, :, :], sg[:, i, :, :], ALU.mult))
                            step.settle()
                            dve.wait_ge(evac_dve, v0 + n * 4 + i)
                            tt(m, m, m_tmp, ALU.add).then_inc(evac_dve, 1)
                            dve.wait_ge(evac_dve, v0 + n * 4 + i + 1)
                    step.leave(NB, 3)
                dve.sem_inc(rows_ready, 1)
                split_T(3 + l * 2, hf_m)
                with dve.Fori(0, NB // 2) as j:
                    for i in range(2):
                        G = base + L_O + j * 2 + i
                        advance(G)
                        residual(G, i, j * 2 + i, False)
                dve.wait_ge(evac_dve, v0 + V_PER)
                end_section()
                step.leave(LAYERS, LAYER_STEPS)


def constants():
    s = np.arange(S)
    con = np.zeros((P, NCON), np.float32)

    def put(name, v):
        con[:, CON[name][0]:CON[name][1]] = np.asarray(v, np.float64).reshape(P, -1)

    p = np.arange(P)
    put("ident", np.eye(P))
    put("ones", np.ones((P, P)))
    put("sel", np.broadcast_to(np.arange(P + SUB) % SUB == 0, (P, P + SUB)))
    decay = np.zeros((P, 2, NH, P))
    for h in range(NH):
        g = 1.0 - 2.0 ** (-5.0 - h)
        sp_, tp = p[:, None], p[None, :]
        decay[:, 0, h] = np.where(sp_ // CHUNK <= tp // CHUNK, g ** np.abs(tp - sp_), 0.0)
        decay[:, 1, h] = g ** (tp + P - sp_)
    put("decay", decay * float(HD) ** -0.5)
    t = s.reshape(TB, P).T
    put("visible", np.where(s[None, None, :] // CHUNK <= t[:, :, None] // CHUNK, 0.0, HIDDEN))
    put("same", (p[:, None] // SUB == p[None, :] // SUB) & (p[:, None] <= p[None, :]))
    inv = np.float32(10000.0) ** (-np.arange(0, HD, 2, dtype=np.float32) / HD)
    ang = (t[:, :, None].astype(np.float32) * inv.astype(np.float32)).astype(np.float64)
    put("cos", np.cos(ang))
    put("sin", np.sin(ang))

    con1 = np.zeros((P, NCON1), np.float32)
    con1[:, 0:TB * S] = np.where(s[None, None, :] <= t[:, :, None], 0.0, FAR).reshape(P, -1)
    con1[:, TB * S:2 * TB * S] = (t[:, :, None] <= s[None, None, :]).reshape(P, -1)
    row = np.zeros((P, 8, P))
    for h in range(8):
        row[h, h] = 1.0
    con1[:, 2 * TB * S:] = row.reshape(P, -1)

    band = np.zeros((P, TB, 4, S), np.float32)
    for g, win in enumerate(POOL_WINDOWS):
        lag = s[None, None, :] - t[:, :, None]
        band[:, :, g, :] = (np.where((lag >= 0) & (lag < win), 1.0 / np.minimum(s + 1, win), 0.0)
                            - (lag == 0))
    return con, con1, band.reshape(P, -1)


def column_tiles(w):
    k, n = w.shape
    return w.reshape(k // (KC * P), KC, P, n // NW, NW).transpose(3, 0, 2, 1, 4).reshape(-1, P, KC * NW)


def chunks(v):
    return v.reshape(-1, P).T


def kernel(**inputs):
    import concourse.bacc as bacc
    from concourse.bass_utils import run_bass_kernel_spmd

    a = {k: np.asarray(v) for k, v in inputs.items()}
    w1 = a["w_in"][0]
    q, k, v, x_, y_ = 512, 1536, 2560, 3592, 4104
    starts = (q, k, v, q + NW, k + NW, v + NW, 0, x_, y_)
    stream = [column_tiles(a["w_mem_kv_2"][l]) for l in range(LAYERS)]
    stream += [column_tiles(w1[:, c:c + NW]) for c in starts]
    stream += [column_tiles(a["w_out"][0])]

    def ff(name, j):
        return column_tiles(a[name][0][:, j * NW:(j + 1) * NW])

    for j in range(NFF + 1):
        if j < NFF:
            stream += [ff("w_ffn_gate", j), ff("w_ffn_up", j)]
        if j:
            stream += [column_tiles(a["w_ffn_down"][0][(j - 1) * NW:j * NW])]
    small = []
    for l in range(LAYERS):
        w2 = a["w_in_2"][l]
        sizes = (512, 512, 512, 512, 512, 72, 512, 512, 512, 512, 512, 512, 512, 512, 512, 512)
        at = np.concatenate([[0], np.cumsum(sizes)])
        for i in range(16):
            part = w2[:, at[i]:at[i + 1]]
            if i == 5:
                small.append(part.reshape(KD, P, SMALL).transpose(1, 0, 2).reshape(P, -1))
            else:
                stream.append(column_tiles(part))
        gates = w2[:, at[-1]:]
        for n in range(NB):
            for b in range(4):
                c = b * D + n * NW
                stream.append(column_tiles(gates[:, c:c + NW]))
            for b in range(4):
                stream.append(column_tiles(a["w_branch_2"][l, b][:, n * NW:(n + 1) * NW]))
        stream.append(column_tiles(a["w_out_2"][l]))
    stream.append(np.zeros((RING, P, KC * NW), np.float32))

    vec = np.concatenate(
        [chunks(a["c"][0]), chunks(a["g_mix"][0]), chunks(a["g_ffn"][0]), chunks(a["final_g"]),
         chunks(a["pool_scale"][0]),
         a["lru_conv_w"][0].reshape(4, 4, P).transpose(2, 1, 0).reshape(P, 16),
         chunks(a["lru_conv_b"][0]), chunks(a["lru_ba"][0]), chunks(a["lru_bi"][0]), chunks(a["lru_lambda"][0]),
         a["ffn_conv_w"][0].reshape(3, FF // P, P).transpose(2, 1, 0).reshape(P, -1),
         chunks(a["ffn_conv_b"][0]), chunks(a["lb_logits_2"]), chunks(a["qk_norm_g_2"][:, 3]), chunks(a["b_ada"][0])],
        axis=1)
    lvec = np.stack([np.concatenate([chunks(a["norm_g_2"][l]), chunks(a["qk_norm_g_2"][l]),
                                     chunks(a["ret_norm_g_2"][l]), chunks(a["hgrn_norm_g_2"][l])], axis=1)
                     for l in range(LAYERS)])
    con, con1, band = constants()
    arrays = {
        "x": a["x"][0].reshape(TB, P, D).transpose(1, 0, 2),
        "mem_T": a["mem_2"][0].T.reshape(KD, P, S).transpose(1, 0, 2),
        "w": np.concatenate(stream),
        "w_ada": a["w_ada"][0].reshape(KD, P, ADA),
        "w_f": w1[:, 3584:3592].reshape(KD, P, 8).transpose(1, 0, 2),
        "b_f": a["b_f"][0],
        "pool_w": a["pool_w"][0].transpose(1, 0, 2),
        "lru_w": np.stack([a["lru_wa"][0], a["lru_wi"][0]]).transpose(2, 0, 1, 3),
        "small_w": np.stack(small),
        "vec": vec, "lvec": lvec, "con": con, "con1": con1, "band": band.reshape(P, TB, 4, S),
    }
    arrays = {n: np.ascontiguousarray(v) for n, v in arrays.items()}
    nc = bacc.Bacc("TRN2", target_bir_lowering=False, num_devices=1)
    t = {n: nc.dram_tensor(n, v.shape, mybir.dt.from_np(v.dtype), kind="ExternalInput").ap()
         for n, v in arrays.items()}
    t["out"] = nc.dram_tensor("out", (P, TB, D), F32, kind="ExternalOutput").ap()
    build(nc, t)
    r = run_bass_kernel_spmd(nc, [arrays], core_ids=[0])
    return r.results[0]["out"].transpose(1, 0, 2).reshape(1, S, D)
```
